# Optimizing a Trainium2 kernel written in Bass

```python
import math
import jax, jax.numpy as jnp
from jax import lax
import numpy as np

D_MODEL = 1024
BATCH = 1
SEQ = 512
DEPTH = 2
DEC_BATCH = 8
DEC_SEQ = 1
PAST_LEN = 4096
PAGE_SIZE = 128

N_MIXERS = 2
N_SSD_LAYERS = (DEPTH + N_MIXERS - 1) // N_MIXERS
N_SC_LAYERS = DEPTH // N_MIXERS
SSD_EXPAND = 2
D_INNER = SSD_EXPAND * D_MODEL
SSD_HEAD_DIM = 64
SSD_HEADS = D_INNER // SSD_HEAD_DIM
SSD_GROUPS = 4
D_STATE = 128
SSD_CONV_K = 4
SSD_CONV_DIM = D_INNER + 2 * SSD_GROUPS * D_STATE
SSD_IN_DIM = D_INNER + SSD_CONV_DIM + SSD_HEADS
CHUNK = 128
SC_EXPAND = 2
D_SC = SC_EXPAND * D_MODEL
SC_CONV_K = 3
SC_IN_DIM = 4 * D_SC
EPS = 1e-5

kernel_name = "ssd_shortconv_hybrid_step"

def rmsnorm(x, w):
    xf = x.astype(jnp.float32)
    out = xf * lax.rsqrt(jnp.mean(xf * xf, axis=-1, keepdims=True) + EPS)
    return (out * w.astype(jnp.float32)).astype(x.dtype)

def grouped_rmsnorm(y, w, groups):
    b, L, d = y.shape
    yf = y.astype(jnp.float32).reshape(b, L, groups, d // groups)
    yf = yf * lax.rsqrt(jnp.mean(yf * yf, axis=-1, keepdims=True) + EPS)
    return (yf.reshape(b, L, d) * w.astype(jnp.float32)).astype(y.dtype)

def causal_dwconv(u, buf, w):
    K = w.shape[0]
    L = u.shape[1]
    ext = jnp.concatenate([buf.astype(u.dtype), u], axis=1)
    out = ext[:, 0:L] * w[0]
    for k in range(1, K):
        out = out + ext[:, k:k + L] * w[k]
    return out, ext[:, L:]

def ssd_chunked(x, dt, A, Bm, Cm, h0):
    b, L, H, P = x.shape
    G, N = Bm.shape[2], Bm.shape[3]
    E = H // G
    Q = math.gcd(L, CHUNK)
    nc = L // Q
    f32 = jnp.float32
    a_cum = jnp.cumsum((dt * A).reshape(b, nc, Q, H), axis=2)
    xd = (x.astype(f32) * dt[..., None]).reshape(b, nc, Q, G, E, P)
    Bc = Bm.astype(f32).reshape(b, nc, Q, G, N)
    Cc = Cm.astype(f32).reshape(b, nc, Q, G, N)
    causal = jnp.tril(jnp.ones((Q, Q), dtype=bool))[None, None, :, :, None]
    seg = a_cum[:, :, :, None, :] - a_cum[:, :, None, :, :]
    Lmat = jnp.exp(jnp.where(causal, seg, -jnp.inf)).reshape(b, nc, Q, Q, G, E)
    CB = jnp.einsum("bclgn,bcsgn->bclsg", Cc, Bc)
    y_diag = jnp.einsum("bclsge,bcsgep->bclgep", CB[..., None] * Lmat, xd)
    decay_to_end = jnp.exp(a_cum[:, :, -1:, :] - a_cum).reshape(b, nc, Q, G, E)
    chunk_states = jnp.einsum("bcsgn,bcsge,bcsgep->bcgepn", Bc, decay_to_end, xd).reshape(b, nc, H, P, N)
    chunk_decay = jnp.exp(a_cum[:, :, -1, :])

    def step(h, inp):
        s, d = inp
        return h * d[:, :, None, None] + s, h

    h_final, h_prev = lax.scan(step, h0.astype(f32),
                               (jnp.moveaxis(chunk_states, 1, 0), jnp.moveaxis(chunk_decay, 1, 0)))
    h_prev = jnp.moveaxis(h_prev, 0, 1).reshape(b, nc, G, E, P, N)
    y_off = jnp.einsum("bclgn,bcgepn,bclge->bclgep", Cc, h_prev,
                       jnp.exp(a_cum).reshape(b, nc, Q, G, E))
    y = (y_diag + y_off).reshape(b, L, H, P)
    return y.astype(x.dtype), h_final.astype(h0.dtype)

def ssd_mixer(h, conv_buf, ssm_state, w_in, conv_w, conv_b, dt_bias, A_log, Dskip, norm_w, w_out):
    b, L, _ = h.shape
    proj = h @ w_in
    z = proj[..., :D_INNER]
    xBC = proj[..., D_INNER:D_INNER + SSD_CONV_DIM]
    dt = proj[..., D_INNER + SSD_CONV_DIM:]
    xBC, new_buf = causal_dwconv(xBC, conv_buf, conv_w)
    xBC = jax.nn.silu(xBC + conv_b)
    xs = xBC[..., :D_INNER].reshape(b, L, SSD_HEADS, SSD_HEAD_DIM)
    Bm = xBC[..., D_INNER:D_INNER + SSD_GROUPS * D_STATE].reshape(b, L, SSD_GROUPS, D_STATE)
    Cm = xBC[..., D_INNER + SSD_GROUPS * D_STATE:].reshape(b, L, SSD_GROUPS, D_STATE)
    dt = jax.nn.softplus((dt + dt_bias).astype(jnp.float32))
    A = -jnp.exp(A_log.astype(jnp.float32))
    y, new_state = ssd_chunked(xs, dt, A, Bm, Cm, ssm_state)
    y = y + Dskip[:, None] * xs
    y = y.reshape(b, L, D_INNER) * jax.nn.silu(z)
    y = grouped_rmsnorm(y, norm_w, SSD_GROUPS)
    return y @ w_out, new_buf, new_state

def short_conv_mixer(h, buf, w_in, conv_w, w_out):
    proj = h @ w_in
    bg = proj[..., :D_SC]
    cg = proj[..., D_SC:2 * D_SC]
    xin = proj[..., 2 * D_SC:3 * D_SC]
    z = proj[..., 3 * D_SC:]
    conv, new_buf = causal_dwconv(cg * xin, buf, conv_w)
    y = bg * conv * jax.nn.silu(z)
    return y @ w_out, new_buf

def setup_inputs(seed: int = 0) -> dict:
    key = jax.random.key(seed)
    ks = jax.random.split(key, 20)
    f32 = jnp.float32
    nrm = lambda k, s, sc: jax.random.normal(k, s, f32) * sc
    dt_init = jnp.exp(jax.random.uniform(ks[9], (N_SSD_LAYERS, SSD_HEADS), f32,
                                         minval=math.log(1e-3), maxval=math.log(1e-1)))
    return {
        "x_prompt": nrm(ks[0], (BATCH, SEQ, D_MODEL), 1.0),
        "x_sample": nrm(ks[1], (DEC_BATCH, DEC_SEQ, D_MODEL), 1.0),
        "state_ssm": nrm(ks[2], (N_SSD_LAYERS, DEC_BATCH, SSD_HEADS, SSD_HEAD_DIM, D_STATE), 0.3),
        "state_ssm_conv": nrm(ks[3], (N_SSD_LAYERS, DEC_BATCH, SSD_CONV_K - 1, SSD_CONV_DIM), 1.0),
        "state_sconv": nrm(ks[4], (N_SC_LAYERS, DEC_BATCH, SC_CONV_K - 1, D_SC), 1.0),
        "norm_w": 1.0 + nrm(ks[5], (DEPTH, D_MODEL), 0.02),
        "final_norm_w": 1.0 + nrm(ks[6], (D_MODEL,), 0.02),
        "ssd_w_in": nrm(ks[7], (N_SSD_LAYERS, D_MODEL, SSD_IN_DIM), D_MODEL ** -0.5),
        "ssd_conv_w": nrm(ks[8], (N_SSD_LAYERS, SSD_CONV_K, SSD_CONV_DIM), SSD_CONV_K ** -0.5),
        "ssd_conv_b": nrm(ks[10], (N_SSD_LAYERS, SSD_CONV_DIM), 0.02),
        "ssd_dt_bias": dt_init + jnp.log(-jnp.expm1(-dt_init)),
        "ssd_A_log": jnp.log(jax.random.uniform(ks[11], (N_SSD_LAYERS, SSD_HEADS), f32, minval=1.0, maxval=16.0)),
        "ssd_D": 1.0 + nrm(ks[12], (N_SSD_LAYERS, SSD_HEADS), 0.02),
        "ssd_norm_w": 1.0 + nrm(ks[13], (N_SSD_LAYERS, D_INNER), 0.02),
        "ssd_w_out": nrm(ks[14], (N_SSD_LAYERS, D_INNER, D_MODEL), D_INNER ** -0.5),
        "sc_w_in": nrm(ks[15], (N_SC_LAYERS, D_MODEL, SC_IN_DIM), D_MODEL ** -0.5),
        "sc_conv_w": nrm(ks[16], (N_SC_LAYERS, SC_CONV_K, D_SC), SC_CONV_K ** -0.5),
        "sc_w_out": nrm(ks[17], (N_SC_LAYERS, D_SC, D_MODEL), D_SC ** -0.5),
    }

def reference(x_prompt, x_sample, state_ssm, state_ssm_conv, state_sconv, norm_w, final_norm_w,
              ssd_w_in, ssd_conv_w, ssd_conv_b, ssd_dt_bias, ssd_A_log, ssd_D, ssd_norm_w, ssd_w_out,
              sc_w_in, sc_conv_w, sc_w_out):
    bp = x_prompt.shape[0]
    dt_ = x_prompt.dtype
    yp, ys = x_prompt, x_sample
    ssm_p, conv_p, sc_p = [], [], []
    ssm_s, conv_s, sc_s = [], [], []
    for i in range(DEPTH):
        j = i // N_MIXERS
        if i % N_MIXERS == 0:
            params = (ssd_w_in[j], ssd_conv_w[j], ssd_conv_b[j], ssd_dt_bias[j], ssd_A_log[j],
                      ssd_D[j], ssd_norm_w[j], ssd_w_out[j])
            zero_buf = jnp.zeros((bp, SSD_CONV_K - 1, SSD_CONV_DIM), dt_)
            zero_h = jnp.zeros((bp, SSD_HEADS, SSD_HEAD_DIM, D_STATE), dt_)
            out_p, cb_p, h_p = ssd_mixer(rmsnorm(yp, norm_w[i]), zero_buf, zero_h, *params)
            out_s, cb_s, h_s = ssd_mixer(rmsnorm(ys, norm_w[i]), state_ssm_conv[j], state_ssm[j], *params)
            yp = yp + out_p
            ys = ys + out_s
            ssm_p.append(h_p); conv_p.append(cb_p)
            ssm_s.append(h_s); conv_s.append(cb_s)
        else:
            zero_buf = jnp.zeros((bp, SC_CONV_K - 1, D_SC), dt_)
            out_p, b_p = short_conv_mixer(rmsnorm(yp, norm_w[i]), zero_buf, sc_w_in[j], sc_conv_w[j], sc_w_out[j])
            out_s, b_s = short_conv_mixer(rmsnorm(ys, norm_w[i]), state_sconv[j], sc_w_in[j], sc_conv_w[j], sc_w_out[j])
            yp = yp + out_p
            ys = ys + out_s
            sc_p.append(b_p)
            sc_s.append(b_s)
    y_prompt = rmsnorm(yp, final_norm_w)
    y_sample = rmsnorm(ys, final_norm_w)
    new_ssm_p = jnp.stack(ssm_p)
    new_ssm_conv_p = jnp.stack(conv_p)
    new_sconv_p = jnp.stack(sc_p)
    new_ssm_s = jnp.stack(ssm_s)
    new_ssm_conv_s = jnp.stack(conv_s)
    new_sconv_s = jnp.stack(sc_s)
    return (y_prompt, y_sample, new_ssm_p, new_ssm_conv_p, new_sconv_p, new_ssm_s, new_ssm_conv_s, new_sconv_s)


_drawn_inputs = setup_inputs


def setup_inputs(seed=0):
    import zlib

    import numpy as np

    out = dict(_drawn_inputs(seed))
    spreads = {}
    factors = {}
    for name, (base, spread) in spreads.items():
        noise = np.random.default_rng([zlib.crc32(name.encode()), seed]).standard_normal(out[name].shape)
        drawn = base * np.exp(spread * noise) if base else spread * noise
        out[name] = __import__('jax').numpy.asarray(drawn.astype(out[name].dtype))
    for name, factor in factors.items():
        out[name] = (out[name] * factor).astype(out[name].dtype)
    return out
```

```python
from contextlib import ExitStack

import concourse.bass as bass
from concourse import mybir

F32 = mybir.dt.float32
F32R = mybir.dt.float32r
ALU = mybir.AluOpType
ACT = mybir.ActivationFunctionType
AX = mybir.AxisListType.X
ds = bass.ds

P = 128
D = 1024
SEQ = 512
NB = 8
T = SEQ + NB
TH = T // 2
KT = D // P
DI = 2048
HEADS, HD, GROUPS, NS = 32, 64, 4, 128
Q = 128
NC = SEQ // Q
XBC = DI + 2 * GROUPS * NS
TILES = DI // P
STEPS = TILES // GROUPS
CT_TILES = XBC // P
EPS = 1e-5

TAPS0, TAPS1 = 4, 3
RAW, SLOT = 2, 4
PRE0, PRE1 = TAPS0 - 1, TAPS1 - 1
EXT0 = PRE0 + SEQ + NB * TAPS0
EXT1 = PRE1 + SEQ + NB * TAPS1
CONV0, CONV1 = EXT0 - PRE0, EXT1 - PRE1
DEC0, DEC1 = PRE0 + SEQ, PRE1 + SEQ
TAIL0, TAIL1 = PRE0 + NB, PRE1 + NB

ORDER = ["B", "C", "x0", "x1", "z0", "x2", "z1", "x3", "z2", "z3"]
CONVED = ["B", "C", "x0", "x1", "x2", "x3"]
OUT0 = len(ORDER) * GROUPS
IN1 = OUT0 + 16
OUT1 = IN1 + 4 * TILES
CHUNKS = OUT1 + 16


def hybrid_step(nc, ins, outs):
    x_prompt, x_sample = ins["x_prompt"], ins["x_sample"]

    with ExitStack() as ctx:
        def sb(name, shape, dt=F32):
            return ctx.enter_context(nc.sbuf_tensor(name, shape, dt))

        def sem(name):
            return ctx.enter_context(nc.semaphore(name))

        bank = [ctx.enter_context(nc.psum_tensor(f"bank{i}", [P, 512], F32)) for i in range(8)]

        xT = sb("xT", [P, KT, T])
        hhi = sb("hhi", [P, KT, T], F32R)
        hlo = sb("hlo", [P, KT, T], F32R)
        raw = sb("raw", [P, RAW, 1024])
        whi = sb("whi", [P, SLOT, 1024], F32R)
        wlo = sb("wlo", [P, SLOT, 1024], F32R)
        ybuf = sb("ybuf", [P, TILES, T])
        ext = sb("ext", [P, 2, EXT0])
        acc = sb("acc", [P, CONV0])
        thx = sb("thx", [P, CONV0])
        xs = sb("xs", [P, 2, CONV0])
        BT = sb("BT", [P, CONV0])
        CT = sb("CT", [P, CONV0])
        Bs = sb("Bs", [P, NC, NS])
        CBm = sb("CBm", [P, NC, Q])
        xd = sb("xd", [P, NC, P])
        xdd = sb("xdd", [P, NC, P])
        abc = sb("abc", [P, 2, SEQ])
        em = sb("em", [P, 2, SEQ])
        ech = sb("ech", [P, SEQ])
        hs = sb("hs", [P, NC, P])
        yob = sb("yob", [P, SEQ - Q])
        finb = sb("finb", [P, NS])
        st = sb("st", [P, 2, NB * NS])
        tdec = sb("tdec", [P, NB, NS])
        bcbc = sb("bcbc", [P, NB, 2, NS])
        bcd = sb("bcd", [NB, 2, NS])
        dtx = sb("dtx", [P, NB])
        yr = sb("yr", [P, NB])
        zh = sb("zh", [P, 2, T])
        th = sb("th", [P, T])
        sqb = sb("sqb", [P, T])
        sqs = sb("sqs", [P, GROUPS, T])
        ident = sb("ident", [P, P])
        mask = sb("mask", [P, Q])
        ones = sb("ones", [P, P])
        colA = sb("colA", [P, P])
        colB = sb("colB", [P, 80])
        cst0 = sb("cst0", [P, CT_TILES, NB, PRE0])
        cst1 = sb("cst1", [P, TILES, NB, PRE1])
        tail0 = sb("tail0", [P, TAIL0, CT_TILES])
        dbc = sb("dbc", [P, HEADS])
        dch = sb("dch", [P, TILES])
        hcol = sb("hcol", [HEADS, 4])
        sm = sb("sm", [HEADS, 4 + 2 * NB])
        acol = sb("acol", [P, NC, HEADS])
        dtcol = sb("dtcol", [P, NC, HEADS])
        dte = sb("dte", [P, NC, HEADS])
        cdbc = sb("cdbc", [P, NC, HEADS])
        dtch = sb("dtch", [P, TILES, NB])
        dcch = sb("dcch", [P, TILES, NB])
        ssq = sb("ssq", [P, 8])
        eps = sb("eps", [P, 1])

        flat = ybuf[:, :, :].rearrange("p a b -> p (a b)")
        x_nat = [flat[:, t * D:(t + 1) * D] for t in range(4)] + [flat[0:NB, 4 * D:5 * D]]
        cs_nat = flat[0:NB * PRE0, 5 * D:5 * D + XBC]
        ss_nat = st[0:NB * PRE1, :, :].rearrange("p a b -> p (a b)")
        htmp = [acc[:, 0:T], thx[:, 0:T]]
        emf = em[:, :, :].rearrange("p a b -> p (a b)")
        tdf = tdec[:, :, :].rearrange("p a b -> p (a b)")
        bcf = bcbc[:, :, :, :].rearrange("p a b c -> p (a b c)")
        dtv, dta, dte_, dtw = (bcf[0:HEADS, 0:T], bcf[0:HEADS, T:2 * T], bcf[0:HEADS, 2 * T:3 * T],
                               tdf[0:HEADS, 0:T])
        dtl, dtT, aT = zh[0:HEADS, 0, :], zh[0:HEADS, 1, :], th[0:HEADS, 0:SEQ]
        sqj = emf[:, 0:D]
        xdf = xd[:, :, :].rearrange("p a b -> p (a b)")
        rowsA, rowsB = xdf[:, 0:P], xdf[0:80, P:2 * P]
        dwr = abc[:, 0, 0:KT * HEADS].rearrange("p (k h) -> p k h", h=HEADS)
        dwh, dwl = (w[:, SLOT - 1, 0:KT * HEADS].rearrange("p (k h) -> p k h", h=HEADS) for w in (whi, wlo))
        SMN = 4 + 2 * NB
        smbc = emf[:, 0:HEADS * SMN].rearrange("p (h v) -> p h v", v=SMN)
        tb0 = emf[0:96, 0:3 * P].rearrange("p (i c) -> p i c", c=P)
        tb1 = emf[0:80, 3 * P:5 * P].rearrange("p (i c) -> p i c", c=P)
        tail1 = cst0[:, :, :, :].rearrange("p t b k -> p (t b k)")[:, 0:TAIL1 * TILES].rearrange("p (r t) -> p r t", t=TILES)
        rb0 = sqb

        def cw0(k, t):
            return colA[:, ds(k * CT_TILES + t, 1)]

        def cb0(t):
            return colA[:, ds(TAPS0 * CT_TILES + t, 1)]
        n0 = TAPS0 * CT_TILES + CT_TILES
        n1, nf, ng, c1 = 0, KT, 2 * KT, 2 * KT + TILES

        a_dram = nc.dram_tensor("a_rows", [HEADS, SEQ], F32, kind="Internal").ap()
        sm_dram = nc.dram_tensor("small_rows", [HEADS, 4 + 2 * NB], F32, kind="Internal").ap()
        bc_dram = nc.dram_tensor("bc_rows", [GROUPS, NB, 2 * NS], F32, kind="Internal").ap()

        w_in0 = ins["ssd_w_in"][0].rearrange("(k p) n -> p k n", p=P)
        w_out0 = ins["ssd_w_out"][0].rearrange("(k p) n -> p k n", p=P)
        w_in1 = ins["sc_w_in"][0].rearrange("(k p) n -> p k n", p=P)
        w_out1 = ins["sc_w_out"][0].rearrange("(k p) n -> p k n", p=P)
        st_in = ins["state_ssm"][0].rearrange("b h p n -> (h p) b n")
        st_out = outs["new_ssm_s"][0].rearrange("b h p n -> (h p) b n")
        fin_out = outs["new_ssm_p"][0, 0].rearrange("h p n -> (h p) n")

        x_in = [sem(f"x_in{t}") for t in range(5)]
        par_in = sem("par_in")
        cs_in = sem("cs_in")
        dtw_in = sem("dtw_in")
        raw_in = [sem(f"raw_in{s}") for s in range(SLOT)]
        hi_done = sem("hi_done")
        lo_done = sem("lo_done")
        proj_done = sem("proj_done")
        proj_free = sem("proj_free")
        consts = sem("consts")
        par_t, par_c = sem("par_t"), sem("par_c")
        ssq_done, rms_done, rcp_done, diag_done = (sem(n) for n in ("ssq_done", "rms_done", "rcp_done", "diag_done"))
        xt_done, xt_out = sem("xt_done"), sem("xt_out")
        rb_done, rb_out = sem("rb_done"), sem("rb_out")
        cs_t, cs_c = sem("cs_t"), sem("cs_c")
        h_full, h_hi, h_lo = sem("h_full"), sem("h_hi"), sem("h_lo")
        dtw_hi, dtw_lo, dt_mm = sem("dtw_hi"), sem("dtw_lo"), sem("dt_mm")
        dt_v, dt_s = sem("dt_v"), sem("dt_s")
        a_out, sm_out, sm_in = sem("a_out"), sem("sm_out"), sem("sm_in")
        col_t = sem("col_t")
        tap, conv_done, tanh_done, silu_done = sem("tap"), sem("conv_done"), sem("tanh_done"), sem("silu_done")
        tb_done, bs_done, cb_done, cbm_done = sem("tb_done"), sem("bs_done"), sem("cb_done"), sem("cbm_done")
        bct_done, bcd_done, bcd_out, bcbc_in = sem("bct_done"), sem("bcd_done"), sem("bcd_out"), sem("bcbc_in")
        t_done, xd_done, xdd_done = sem("t_done"), sem("xd_done"), sem("xdd_done")
        seg_done = sem("seg_done")
        abc_in, e_done, ech_done, m_done = sem("abc_in"), sem("e_done"), sem("ech_done"), sem("m_done")
        s_done, sd_done, rec, fin_t, o_done = sem("s_done"), sem("sd_done"), sem("rec"), sem("fin_t"), sem("o_done")
        fin_done, fin_st = sem("fin_done"), sem("fin_st")
        yd_done, yo_done, y_done = sem("yd_done"), sem("yo_done"), sem("y_done")
        st_ld, st_st = [sem(f"st_ld{s}") for s in range(2)], [sem(f"st_st{s}") for s in range(2)]
        dtx_done, t1_done, dh_done, st_new, t2_done = (sem(n) for n in ("dtx_done", "t1_done", "dh_done", "st_new", "t2_done"))
        yr_done, ydec_done = sem("yr_done"), sem("ydec_done")
        zt_done, sz_done, gate_done, sq_done, sqs_done = (sem(n) for n in ("zt_done", "sz_done", "gate_done", "sq_done", "sqs_done"))
        tail_t, tail_c, tail_st = sem("tail_t"), sem("tail_c"), sem("tail_st")
        stat_mm, rs_sqrt, rs_done, ys_done = sem("stat_mm"), sem("rs_sqrt"), sem("rs_done"), sem("ys_done")
        y_hi, y_lo = sem("y_hi"), sem("y_lo")
        out_mm, out_evac, evac_a = sem("out_mm"), sem("out_evac"), sem("evac_a")
        u_done, cg_free, xin_free, z_free, bg_free = (sem(n) for n in ("u_done", "cg_free", "xin_free", "z_free", "bg_free"))
        cs1_done, tail1_done, tap1, sl_done, slr_done, c2_done = (sem(n) for n in ("cs1_done", "tail1_done", "tap1", "sl_done", "slr_done", "c2_done"))
        wf_done, fin_tr, fin_ev, col_sq, col_rms, col_rcp, y_st = (sem(n) for n in ("wf_done", "fin_tr", "fin_ev", "col_sq", "col_rms", "col_rcp", "y_st"))
        direct_st = sem("direct_st")

        turnstile, turnstile_p = sem("turnstile"), sem("turnstile_p")

        block = ctx.enter_context(nc.Block())

        def dec4(row):
            return row[:, DEC0:DEC0 + NB * TAPS0].rearrange("p (b k) -> p b k", k=TAPS0)

        def dec_conv(row):
            return row[:, DEC0:CONV0:TAPS0]

        def group_half(G, gg):
            return 2 * G + gg

        @block.sync
        def _(sp):
            def load(n, i, src):
                slot = i % RAW
                count = sp.snap(n + (1 + SLOT - RAW))
                sp.wait_ge(hi_done, count)
                sp.sem_inc(turnstile, 1)
                sp.wait_ge(lo_done, count)
                sp.sem_inc(turnstile, 1)
                k = src.shape[1]
                sp.dma_start(raw[:, slot, :].rearrange("p (k n) -> p k n", k=k), src).then_inc(raw_in[slot], 16)

            for t in range(4):
                sp.dma_start(x_nat[t], x_prompt[0, t * P:(t + 1) * P, :]).then_inc(x_in[t], 16)
            sp.dma_start(dwr[:, :, :], w_in0[:, :, DI + XBC:DI + XBC + HEADS]).then_inc(dtw_in, 16)
            with sp.Fori(0, GROUPS // 2) as G:
                for gg in range(2):
                    g = group_half(G, gg)
                    for m, what in enumerate(ORDER):
                        if what == "B":
                            col = g * NS + 2 * DI
                        elif what == "C":
                            col = g * NS + (2 * DI + GROUPS * NS)
                        else:
                            col = g * (STEPS * P) + (int(what[1]) * P + (DI if what[0] == "x" else 0))
                        i = gg * 10 + m
                        load(G * 20 + i, i, w_in0[:, :, ds(sp.snap(col), P)])

            def load_out(base, w):
                with sp.Fori(0, 2) as half:
                    for c in range(8):
                        load(half * 8 + (base + c), c, w[:, 2 * c:2 * c + 2, ds(sp.snap(half * 512), 512)])

            load_out(OUT0, w_out0)
            with sp.Fori(0, TILES) as j:
                for m, part in enumerate((1, 2, 0, 3)):
                    load(j * 4 + (IN1 + m), m, w_in1[:, :, ds(sp.snap(j * P + part * DI), P)])
            load_out(OUT1, w_out1)

            sp.dma_start(outs["new_ssm_conv_s"][0, :, 0:PRE0 - 1, :], ins["state_ssm_conv"][0, :, 1:PRE0, :]).then_inc(direct_st, 16)
            sp.dma_start(outs["new_sconv_s"][0, :, 0:PRE1 - 1, :], ins["state_sconv"][0, :, 1:PRE1, :]).then_inc(direct_st, 16)

            sp.wait_ge(tail_c, 1)
            cp = outs["new_ssm_conv_p"][0, 0].rearrange("r (t c) -> (r t) c", c=P)
            csv = outs["new_ssm_conv_s"][0, :, PRE0 - 1, :].rearrange("b (t c) -> b t c", c=P)
            sp.dma_start(cp, tb0[0:72, 0, :]).then_inc(tail_st, 16)
            sp.dma_start(csv[0], tb0[72:96, 0, :]).then_inc(tail_st, 16)
            for b in range(1, NB):
                i, o = (b + 3) // 4, (b + 3) % 4 * CT_TILES
                sp.dma_start(csv[b], tb0[o:o + CT_TILES, i, :]).then_inc(tail_st, 16)
            sp.wait_ge(tail_c, 2)
            sp.dma_start(outs["new_sconv_p"][0, 0].rearrange("r (t c) -> (r t) c", c=P), tb1[0:32, 0, :]).then_inc(tail_st, 16)
            ssv = outs["new_sconv_s"][0, :, PRE1 - 1, :].rearrange("b (t c) -> b t c", c=P)
            for b in range(NB):
                i, o = (b + 2) // 5, (b + 2) % 5 * TILES
                sp.dma_start(ssv[b], tb1[o:o + TILES, i, :]).then_inc(tail_st, 16)

            for t in range(5):
                sp.wait_ge(fin_ev, t + 1)
                sp.wait_ge(evac_a, t + 1)
                if t < 4:
                    sp.dma_start(outs["y_prompt"][0, t * P:(t + 1) * P, :], x_nat[t]).then_inc(y_st, 16)
                else:
                    sp.dma_start(outs["y_sample"][:, 0, :], x_nat[4]).then_inc(y_st, 16)
            sp.wait_ge(y_st, 5 * 16)
            sp.wait_ge(tail_st, 18 * 16)
            sp.wait_ge(direct_st, 2 * 16)

        @block.gpsimd
        def _(pool):
            pool.memset(ident[:, :], 0.0).then_inc(consts, 1)
            pool.memset(mask[:, :], 1.0).then_inc(consts, 1)
            pool.wait_ge(consts, 2)
            pool.affine_select(out=ident[:, :], in_=ident[:, :], compare_op=ALU.not_equal, fill=1.0, base=0,
                               pattern=[[-1, P]], channel_multiplier=1).then_inc(consts, 1)
            pool.affine_select(out=mask[:, :], in_=mask[:, :], compare_op=ALU.is_ge, fill=0.0, base=0,
                               pattern=[[1, Q]], channel_multiplier=-1).then_inc(consts, 1)
            pool.memset(ones[:, :], 1.0).then_inc(consts, 1)
            pool.memset(eps[:, :], EPS).then_inc(consts, 1)
            pool.memset(ext[:, :, 0:PRE0], 0.0).then_inc(consts, 1)
            pool.memset(sqs[:, :, :], 0.0).then_inc(consts, 1)
            pool.sem_inc(lo_done, SLOT)
            pool.sem_inc(sqs_done, 1)

            def low(n, slot, turn):
                pool.wait_ge(hi_done, n + (1 + SLOT))
                pool.wait_ge(raw_in[slot % RAW], turn)
                pool.tensor_tensor(wlo[:, slot, :], raw[:, slot % RAW, :], whi[:, slot, :].bitcast(F32), ALU.subtract).then_inc(lo_done, 1)

            pool.wait_ge(dtw_hi, 1)
            pool.tensor_tensor(dwl[:, :, :], dwr[:, :, :], dwh[:, :, :].bitcast(F32), ALU.subtract).then_inc(dtw_lo, 1)
            for n in range(SLOT):
                if n == SLOT - 1:
                    pool.wait_ge(dt_mm, 1)
                low(n, n, (n // RAW + 1) * 16)

            with pool.Fori(0, GROUPS // 2) as G:
                for gg in range(2):
                    g = group_half(G, gg)

                    def next_low(m):
                        i = gg * 10 + m
                        pool.wait_ge(proj_done, G * 20 + (i + 1))
                        low(G * 20 + (i + SLOT), i % SLOT, G * 160 + ((i + SLOT) // RAW + 1) * 16)

                    def weigh(q):
                        pool.wait_ge(xd_done, g * 4 + (q + 1))
                        scale = dte[:, :, ds(g * 8 + 2 * q, 2)].unsqueeze(3).broadcast_to([P, NC, 2, HD])
                        pool.sem_inc(turnstile_p, 1)
                        pool.tensor_tensor(xdd[:, :, :].rearrange("p c (h d) -> p c h d", h=2),
                                           xd[:, :, :].rearrange("p c (h d) -> p c h d", h=2), scale, ALU.mult).then_inc(xdd_done, 1)

                    def inject(q):
                        pool.wait_ge(dtx_done, g * 4 + (q + 1))
                        if q == 0:
                            pool.wait_ge(bcbc_in, g * 16 + 16)
                        pool.tensor_tensor(tdec[:, :, :], bcbc[:, :, 0, :], dtx[:, :].unsqueeze(2).broadcast_to([P, NB, NS]),
                                           ALU.mult).then_inc(t1_done, 1)

                    def read_out(q):
                        pool.wait_ge(st_new, g * 4 + (q + 1))
                        pool.tensor_tensor(tdec[:, :, :], st[:, q % 2, :].rearrange("p (b n) -> p b n", n=NS),
                                           bcbc[:, :, 1, :], ALU.mult).then_inc(t2_done, 1)

                    def gate(q):
                        pool.wait_ge(sz_done, g * 4 + (q + 2))
                        pool.wait_ge(y_done, g * 4 + (q + 1))
                        pool.wait_ge(ydec_done, g * 4 + (q + 1))
                        yt = ybuf[:, ds(g * 4 + q, 1), :].squeeze(1)
                        pool.sem_inc(turnstile_p, 1)
                        pool.tensor_tensor(yt, yt, zh[:, q % 2, :], ALU.mult).then_inc(gate_done, 1)

                    def add_squares(q):
                        pool.wait_ge(sq_done, g * 4 + (q + 1))
                        if q > 0:
                            pool.wait_ge(sqs_done, g * 4 + (q + 1))
                        ss = sqs[:, ds(g, 1), :].squeeze(1)
                        pool.sem_inc(turnstile_p, 1)
                        pool.tensor_tensor(ss, ss, sqb[:, :], ALU.add).then_inc(sqs_done, 1)

                    if gg == 0:
                        pass
                    for m in range(4):
                        next_low(m)
                    weigh(0)
                    next_low(4)
                    inject(0)
                    next_low(5)
                    weigh(1)
                    read_out(0)
                    gate(0)
                    next_low(6)
                    add_squares(0)
                    inject(1)
                    next_low(7)
                    weigh(2)
                    read_out(1)
                    gate(1)
                    next_low(8)
                    add_squares(1)
                    inject(2)
                    weigh(3)
                    read_out(2)
                    next_low(9)
                    gate(2)
                    add_squares(2)
                    inject(3)
                    read_out(3)
                    gate(3)
                    add_squares(3)

            with pool.Fori(0, 2) as half:
                for c in range(8):
                    pool.wait_ge(proj_done, half * 8 + (OUT0 + c + 1))
                    low(half * 8 + (OUT0 + c + SLOT), c % SLOT, half * 64 + ((OUT0 + c + SLOT) // RAW + 1) * 16)
            for k in range(KT):
                pool.wait_ge(sq_done, TILES + k + 1)
                if k == 0:
                    pool.wait_ge(ys_done, TILES)
                    pool.tensor_copy(sqs[:, 0, :], sqb[:, :]).then_inc(sqs_done, 1)
                else:
                    pool.wait_ge(sqs_done, TILES + k + 1)
                    pool.tensor_tensor(sqs[:, 0, :], sqs[:, 0, :], sqb[:, :], ALU.add).then_inc(sqs_done, 1)
            with pool.Fori(0, TILES) as j:
                for m in range(4):
                    pool.wait_ge(proj_done, j * 4 + (IN1 + m + 1))
                    low(j * 4 + (IN1 + m + SLOT), m, j * 32 + ((IN1 + m + SLOT) // RAW + 1) * 16)
            for n in range(OUT1, CHUNKS - SLOT):
                pool.wait_ge(proj_done, n + 1)
                low(n + SLOT, n % SLOT, ((n + SLOT) // RAW + 1) * 16)

        @block.scalar
        def _(act):
            act.sem_inc(hi_done, SLOT)
            act.sem_inc(proj_free, 2)
            act.sem_inc(fin_done, 1)
            act.sem_inc(fin_st, 16)
            for s in range(2):
                act.sem_inc(st_st[s], 16)
            act.sem_inc(ech_done, 1)
            act.sem_inc(bcd_out, 16)

            act.dma_start(x_nat[4], x_sample[:, 0, :]).then_inc(x_in[4], 16)
            act.dma_start(rowsA[0:96, :], ins["ssd_conv_w"][0].rearrange("k (t c) -> (k t) c", c=P)).then_inc(par_in, 16)
            act.dma_start(rowsA[96:120, :], ins["ssd_conv_b"][0].rearrange("(t c) -> t c", c=P)).then_inc(par_in, 16)
            act.dma_start(rowsA[120:128, :], ins["norm_w"][0].rearrange("(t c) -> t c", c=P)).then_inc(par_in, 16)
            act.dma_start(rowsB[0:8, :], ins["norm_w"][1].rearrange("(t c) -> t c", c=P)).then_inc(par_in, 16)
            act.dma_start(rowsB[8:16, :], ins["final_norm_w"].rearrange("(t c) -> t c", c=P)).then_inc(par_in, 16)
            act.dma_start(rowsB[16:32, :], ins["ssd_norm_w"][0].rearrange("(t c) -> t c", c=P)).then_inc(par_in, 16)
            act.dma_start(rowsB[32:80, :], ins["sc_conv_w"][0].rearrange("k (t c) -> (k t) c", c=P)).then_inc(par_in, 16)
            act.dma_start(hcol[:, 0:1], ins["ssd_dt_bias"].rearrange("a h -> h a")).then_inc(par_in, 16)
            act.dma_start(hcol[:, 1:2], ins["ssd_A_log"].rearrange("a h -> h a")).then_inc(par_in, 16)
            act.dma_start(dbc[:, :], ins["ssd_D"][0].partition_broadcast(P)).then_inc(par_in, 16)
            act.dma_start(cs_nat, ins["state_ssm_conv"][0].rearrange("b k c -> (b k) c")).then_inc(cs_in, 16)
            act.dma_start(ss_nat, ins["state_sconv"][0].rearrange("b k c -> (b k) c")).then_inc(cs_in, 16)

            def high(n, slot, turn):
                act.wait_ge(raw_in[slot % RAW], turn)
                act.activation(whi[:, slot, :], raw[:, slot % RAW, :], ACT.Copy).then_inc(hi_done, 1)

            for t in range(5):
                rows = P if t < 4 else NB
                act.wait_ge(x_in[t], 16)
                if t > 0:
                    act.wait_ge(ssq_done, t)
                act.activation(sqj[0:rows, :], x_nat[t], ACT.Square, accum_out=ssq[0:rows, t:t + 1]).then_inc(ssq_done, 1)
            act.wait_ge(consts, 8)
            act.wait_ge(ssq_done, 5)
            act.activation(ssq[:, 0:4], ssq[:, 0:4], ACT.Sqrt, scale=1.0 / D, bias=eps[:, 0:1]).then_inc(rms_done, 1)
            act.activation(ssq[0:NB, 4:5], ssq[0:NB, 4:5], ACT.Sqrt, scale=1.0 / D, bias=eps[0:NB, 0:1]).then_inc(rms_done, 1)
            act.wait_ge(dtw_in, 16)
            act.activation(dwh[:, :, :], dwr[:, :, :], ACT.Copy).then_inc(dtw_hi, 1)
            for k in range(KT):
                act.wait_ge(xt_done, k + 1)
                act.activation(xT[:, k, 0:SEQ], bank[k % 4][:, :], ACT.Copy).then_inc(xt_out, 1)
            act.wait_ge(xt_done, KT + 1)
            act.activation(xT[:, :, SEQ:T], bank[4][:, 0:KT * NB].rearrange("p (k b) -> p k b", b=NB), ACT.Copy).then_inc(xt_out, 1)
            for k in range(KT):
                act.wait_ge(h_full, k + 1)
                act.activation(hhi[:, k, :], htmp[k % 2], ACT.Copy).then_inc(h_hi, 1)
                if k % 2 and k < 6:
                    high(k // 2, k // 2, (k // 2 // RAW + 1) * 16)
            act.wait_ge(dt_mm, 1)
            high(SLOT - 1, SLOT - 1, ((SLOT - 1) // RAW + 1) * 16)
            act.wait_ge(cs_t, 3)
            for i in range(2):
                act.activation(cst0[:, i * 12:(i + 1) * 12, :, :].rearrange("p t b k -> p (t b k)"),
                               bank[i][:, 0:288], ACT.Copy).then_inc(cs_c, 1)
            act.activation(cst1[:, :, :, :].rearrange("p t b k -> p (t b k)"), bank[2][:, 0:256], ACT.Copy).then_inc(cs_c, 1)

            act.wait_ge(par_in, 160)
            act.activation(hcol[:, 2:3], hcol[:, 1:2], ACT.Exp).then_inc(dt_s, 1)
            act.wait_ge(dt_v, 2)
            act.activation(dta, dtv, ACT.Abs).then_inc(dt_s, 1)
            act.wait_ge(dt_s, 2)
            act.activation(dte_, dta, ACT.Exp, scale=-1.0).then_inc(dt_s, 1)
            act.wait_ge(dt_v, 4)
            act.activation(dtl, dtw, ACT.Ln).then_inc(dt_s, 1)
            act.wait_ge(dt_v, 11)
            act.activation(sm[:, 4 + NB:4 + 2 * NB], dta[:, SEQ:T], ACT.Exp).then_inc(dt_s, 1)
            act.wait_ge(dt_v, 17)
            act.dma_start(a_dram, aT).then_inc(a_out, 16)
            act.wait_ge(dt_s, 5)
            act.dma_start(sm_dram, sm[:, :]).then_inc(sm_out, 16)
            act.wait_ge(sm_out, 16)
            act.dma_start(smbc[:, :, :], sm_dram.partition_broadcast(P)).then_inc(sm_in, 16)
            act.wait_ge(col_t, 1)
            act.activation(acol[:, :, :].rearrange("p c h -> p (c h)"), bank[7][:, 0:P], ACT.Copy).then_inc(dt_s, 1)
            act.activation(dtcol[:, :, :].rearrange("p c h -> p (c h)"), bank[7][:, P:2 * P], ACT.Copy).then_inc(dt_s, 1)
            act.wait_ge(sm_in, 16)
            act.activation(cdbc[:, :, :], smbc[:, :, 0:4].rearrange("p h c -> p c h"), ACT.Exp).then_inc(dt_s, 1)
            act.wait_ge(dt_v, 18)
            act.activation(dte[:, :, :], dte[:, :, :], ACT.Exp).then_inc(dt_s, 1)
            act.wait_ge(a_out, 16)
            act.wait_ge(dt_s, 9)
            act.wait_ge(dt_v, 24)
            act.wait_ge(cs_c, 3)

            with act.Fori(0, GROUPS // 2) as G:
                for gg in range(2):
                    g = group_half(G, gg)

                    def split_next(m):
                        i = gg * 10 + m
                        high(G * 20 + (i + SLOT), i % SLOT, G * 160 + ((i + SLOT) // RAW + 1) * 16)

                    def evac_conv(m, tile):
                        i = gg * 10 + m
                        e = CONVED.index(ORDER[m])
                        b0, b1 = bank[2 * (m % 2)], bank[2 * (m % 2) + 1]
                        row = ext[:, e % 2, :]
                        act.wait_ge(proj_done, G * 20 + (i + 1))
                        act.activation(row[:, PRE0:PRE0 + TH], b0[:, 0:TH], ACT.Copy)
                        act.activation(row[:, PRE0 + TH:PRE0 + SEQ], b1[:, 0:SEQ - TH], ACT.Copy)
                        act.activation(dec4(row)[:, :, PRE0], b1[:, SEQ - TH:TH], ACT.Copy)
                        act.activation(tail0[:, :, ds(tile, 1)].squeeze(2), b1[:, SEQ - TH - PRE0:TH], ACT.Copy)
                        act.activation(dec4(row)[:, :, 0:PRE0], cst0[:, ds(tile, 1), :, :].squeeze(1), ACT.Copy).then_inc(proj_free, 1)
                        split_next(m)

                    def tanh_conv(e):
                        act.wait_ge(conv_done, g * 6 + (e + 1))
                        act.wait_ge(silu_done, g * 6 + (e + 1))
                        act.activation(thx[:, :], acc[:, :], ACT.Tanh).then_inc(tanh_done, 1)

                    def evac_z(m, q):
                        i = gg * 10 + m
                        b0, b1 = bank[2 * (m % 2)], bank[2 * (m % 2) + 1]
                        act.wait_ge(proj_done, G * 20 + (i + 1))
                        act.activation(zh[:, q % 2, 0:TH], b0[:, 0:TH], ACT.Copy, scale=0.5)
                        act.activation(zh[:, q % 2, TH:T], b1[:, 0:TH], ACT.Copy, scale=0.5).then_inc(proj_free, 1)
                        split_next(m)
                        act.wait_ge(proj_free, G * 20 + (i + 1 + 2))
                        act.wait_ge(sz_done, g * 4 + (q + 1))
                        act.activation(th[:, :], zh[:, q % 2, :], ACT.Tanh).then_inc(zt_done, 1)

                    def load_abc(q):
                        act.wait_ge(ech_done, g * 4 + (q + 1))
                        act.dma_start(abc[:, :, :], a_dram[ds(g * 8 + 2 * q, 2), :].partition_broadcast(P)).then_inc(abc_in, 16)

                    def decay(q):
                        act.wait_ge(abc_in, g * 64 + 16 * (q + 1))
                        act.wait_ge(sd_done, g * 4 + (q + 1))
                        for h in range(2):
                            for c in range(NC):
                                e = act.activation(em[:, h, c * Q:(c + 1) * Q], abc[:, h, c * Q:(c + 1) * Q], ACT.Relu,
                                                   scale=-1.0, bias=acol[:, c, ds(g * 8 + (2 * q + h), 1)])
                        e.then_inc(seg_done, 1)
                        act.wait_ge(seg_done, g * 4 + (q + 1))
                        act.activation(em[:, :, :], em[:, :, :], ACT.Exp, scale=-1.0).then_inc(e_done, 1)

                    def decay_channels(q):
                        act.wait_ge(yo_done, g * 4 + (q + 1))
                        act.activation(ech[0:HD, :], abc[0:HD, 0, :], ACT.Exp)
                        act.activation(ech[HD:P, :], abc[HD:P, 1, :], ACT.Exp).then_inc(ech_done, 1)

                    def final_state(q):
                        act.wait_ge(fin_t, g * 4 + (q + 1))
                        act.wait_ge(fin_st, g * 64 + 16 * (q + 1))
                        act.activation(finb[:, :], bank[5][:, 0:NS], ACT.Copy).then_inc(fin_done, 1)
                        act.wait_ge(fin_done, g * 4 + (q + 2))
                        act.dma_start(fin_out[ds(g * 512 + q * P, P), :], finb[:, :]).then_inc(fin_st, 16)

                    def load_state(q):
                        act.wait_ge(st_st[q % 2], g * 32 + 16 * (q // 2 + 1))
                        act.dma_start(st[:, q % 2, :].rearrange("p (b n) -> p b n", n=NS),
                                      st_in[ds(g * 512 + q * P, P), :, :]).then_inc(st_ld[q % 2], 16)

                    def store_state(q):
                        act.wait_ge(st_new, g * 4 + (q + 1))
                        act.dma_start(st_out[ds(g * 512 + q * P, P), :, :],
                                      st[:, q % 2, :].rearrange("p (b n) -> p b n", n=NS)).then_inc(st_st[q % 2], 16)

                    def squares(q):
                        act.wait_ge(gate_done, g * 4 + (q + 1))
                        act.wait_ge(sqs_done, g * 4 + (q + 1))
                        act.activation(sqb[:, :], ybuf[:, ds(g * 4 + q, 1), :].squeeze(1), ACT.Square).then_inc(sq_done, 1)

                    load_abc(0)
                    evac_conv(0, g + TILES)
                    load_state(0)
                    tanh_conv(0)
                    evac_conv(1, g + (TILES + GROUPS))
                    load_state(1)
                    tanh_conv(1)
                    decay(0)
                    decay_channels(0)
                    load_abc(1)
                    evac_conv(2, g * 4)
                    tanh_conv(2)
                    act.wait_ge(tb_done, g + 1)
                    act.activation(Bs[:, :, :].rearrange("p c n -> p (c n)"), bank[4][:, :], ACT.Copy).then_inc(bs_done, 1)
                    evac_conv(3, g * 4 + 1)
                    act.wait_ge(bcd_done, g + 1)
                    act.dma_start(bc_dram[ds(g, 1), :, :].squeeze(0), bcd[:, :, :].rearrange("b a n -> b (a n)")).then_inc(bcd_out, 16)
                    tanh_conv(3)
                    evac_z(4, 0)
                    act.wait_ge(bcd_out, g * 16 + 32)
                    act.dma_start(bcbc[:, :, :, :].rearrange("p b a n -> p b (a n)"),
                                  bc_dram[ds(g, 1), :, :].squeeze(0).partition_broadcast(P)).then_inc(bcbc_in, 16)
                    decay(1)
                    evac_conv(5, g * 4 + 2)
                    tanh_conv(4)
                    final_state(0)
                    store_state(0)
                    decay_channels(1)
                    load_abc(2)
                    squares(0)
                    evac_z(6, 1)
                    load_state(2)
                    decay(2)
                    evac_conv(7, g * 4 + 3)
                    tanh_conv(5)
                    final_state(1)
                    store_state(1)
                    decay_channels(2)
                    load_abc(3)
                    squares(1)
                    evac_z(8, 2)
                    load_state(3)
                    decay(3)
                    evac_z(9, 3)
                    final_state(2)
                    store_state(2)
                    decay_channels(3)
                    squares(2)
                    final_state(3)
                    squares(3)
                    store_state(3)

            act.wait_ge(tail_t, 1)
            act.activation(tb0[:, 0:2, :], bank[0][0:96, 0:2 * P].rearrange("p (i c) -> p i c", c=P), ACT.Copy)
            act.activation(tb0[0:72, 2, :], bank[0][0:72, 2 * P:3 * P], ACT.Copy).then_inc(tail_c, 1)
            for g in range(GROUPS):
                act.wait_ge(stat_mm, g + 1)
                a, b = bank[(2 * g + 2) % 8], bank[(2 * g + 3) % 8]
                act.activation(sqs[:, g, 0:TH], a[:, 0:TH], ACT.Sqrt, scale=1.0 / 512, bias=eps[:, 0:1])
                act.activation(sqs[:, g, TH:T], b[:, 0:TH], ACT.Sqrt, scale=1.0 / 512, bias=eps[:, 0:1]).then_inc(rs_sqrt, 1)

            def out_phase(base, layer):
                def y_high(r):
                    if layer == 0 and r < TILES:
                        act.wait_ge(ys_done, r + 1)
                    if layer == 1 and r < TILES:
                        act.wait_ge(bg_free, r + 2)
                    act.wait_ge(proj_done, base if r < 8 else base + (r - 8) // 2 + 1)
                    act.activation(hhi[:, r % 8, :], ybuf[:, r % TILES, :], ACT.Copy).then_inc(y_hi, 1)
                for r in range(8):
                    y_high(r)
                for c in range(16):
                    act.wait_ge(proj_done, base + c + 1)
                    n = base + c + SLOT
                    if n < CHUNKS:
                        high(n, n % SLOT, (n // RAW + 1) * 16)
                    if 2 * c + 8 < 32:
                        y_high(2 * c + 8)
                        y_high(2 * c + 9)

            out_phase(OUT0, 0)

            for k in range(KT):
                act.wait_ge(out_evac, 4 + k + 1)
                act.activation(hhi[:, k, :], xT[:, k, :], ACT.Copy, scale=colB[:, n1 + k:n1 + k + 1]).then_inc(h_hi, 1)
                act.wait_ge(sqs_done, TILES + k + 1)
                act.activation(sqb[:, :], xT[:, k, :], ACT.Square).then_inc(sq_done, 1)
            act.wait_ge(stat_mm, GROUPS + 1)
            act.activation(sqs[:, 1, 0:TH], bank[6][:, 0:TH], ACT.Sqrt, scale=1.0 / D, bias=eps[:, 0:1])
            act.activation(sqs[:, 1, TH:T], bank[7][:, 0:TH], ACT.Sqrt, scale=1.0 / D, bias=eps[:, 0:1]).then_inc(rs_sqrt, 1)

            with act.Fori(0, TILES) as j:
                for m in range(4):
                    act.wait_ge(proj_done, j * 4 + (IN1 + m + 1))
                    high(j * 4 + (IN1 + m + SLOT), m, j * 32 + ((IN1 + m + SLOT) // RAW + 1) * 16)
                act.wait_ge(z_free, j + 2)
                act.wait_ge(slr_done, j + 1)
                act.activation(th[:, :], zh[:, 1, :], ACT.Silu).then_inc(sl_done, 1)

            act.wait_ge(tail_t, 2)
            act.activation(tb1[:, :, :], bank[0][0:80, 0:2 * P].rearrange("p (i c) -> p i c", c=P), ACT.Copy).then_inc(tail_c, 1)
            out_phase(OUT1, 1)

            for k in range(KT):
                act.wait_ge(out_evac, 12 + k + 1)
                if k > 0:
                    act.wait_ge(sqs_done, TILES + KT + 1)
                    act.wait_ge(ydec_done, TILES + k)
                act.activation(sqb[:, :], xT[:, k, :], ACT.Square).then_inc(sq_done, 1)
                act.activation(xT[:, k, :], xT[:, k, :], ACT.Copy, scale=colB[:, nf + k:nf + k + 1]).then_inc(wf_done, 1)
            act.wait_ge(col_sq, 1)
            act.activation(ssq[:, 0:4], bank[7][:, 0:4], ACT.Sqrt, scale=1.0 / D, bias=eps[:, 0:1])
            act.activation(ssq[0:NB, 4:5], bank[7][0:NB, 4:5], ACT.Sqrt, scale=1.0 / D, bias=eps[0:NB, 0:1]).then_inc(col_rms, 1)
            act.wait_ge(col_rcp, 1)
            for t in range(5):
                rows = P if t < 4 else NB
                act.wait_ge(fin_tr, t + 1)
                act.activation(x_nat[t][:, 0:512], bank[2 * t % 8][0:rows, :], ACT.Copy, scale=ssq[0:rows, t:t + 1]).then_inc(fin_ev, 1)
            act.wait_ge(fin_st, 16 * 17)
            for s in range(2):
                act.wait_ge(st_st[s], 16 * 9)

        @block.vector
        def _(dve):
            dve.sem_inc(silu_done, 1)
            dve.sem_inc(yo_done, 1)
            dve.sem_inc(yd_done, 1)
            dve.sem_inc(sz_done, 1)
            dve.sem_inc(out_evac, 4)
            for s in (cg_free, xin_free, z_free, bg_free, slr_done):
                dve.sem_inc(s, 1)

            dve.wait_ge(rms_done, 2)
            dve.reciprocal(ssq[:, 0:4], ssq[:, 0:4]).then_inc(rcp_done, 1)
            dve.reciprocal(ssq[0:NB, 4:5], ssq[0:NB, 4:5]).then_inc(rcp_done, 1)
            dve.wait_ge(rcp_done, 2)
            dve.wait_ge(consts, 8)
            for t in range(4):
                dve.tensor_scalar(xdd[:, t, :], ident[:, :], ssq[:, t:t + 1], None, ALU.mult).then_inc(diag_done, 1)
            dve.tensor_scalar(finb[0:NB, 0:NB], ident[0:NB, 0:NB], ssq[0:NB, 4:5], None, ALU.mult).then_inc(diag_done, 1)
            dve.wait_ge(par_t, 1)
            dve.tensor_scalar(colA[:, 0:n0], bank[7][:, 0:n0], 0.5, None, ALU.mult)
            dve.tensor_copy(colA[:, n0:P], bank[7][:, n0:P])
            dve.tensor_copy(colB[:, :], bank[7][:, P:P + 80]).then_inc(par_c, 1)
            dve.wait_ge(par_c, 1)
            dve.wait_ge(rb_done, 1)
            dve.tensor_copy(rb0[:, 0:SEQ], bank[5][:, :])
            dve.tensor_copy(rb0[:, SEQ:T], bank[6][:, 0:NB]).then_inc(rb_out, 1)
            dve.wait_ge(rb_out, 1)
            dve.wait_ge(xt_out, KT + 1)
            for k in range(KT + 1):
                if 2 <= k < KT:
                    dve.wait_ge(h_lo, k - 1)
                if k < KT:
                    dve.scalar_tensor_tensor(htmp[k % 2], xT[:, k, :], colA[:, n0 + k:n0 + k + 1], rb0[:, :],
                                             ALU.mult, ALU.mult).then_inc(h_full, 1)
                if k > 0:
                    dve.wait_ge(h_hi, k)
                    dve.wait_ge(h_full, k)
                    dve.tensor_tensor(hlo[:, k - 1, :], htmp[(k - 1) % 2], hhi[:, k - 1, :].bitcast(F32), ALU.subtract).then_inc(h_lo, 1)

            dve.wait_ge(par_in, 160)
            dve.wait_ge(dt_mm, 1)
            dve.tensor_scalar(dtv[:, 0:TH], bank[6][0:HEADS, 0:TH], hcol[:, 0:1], None, ALU.add).then_inc(dt_v, 1)
            dve.tensor_scalar(dtv[:, TH:T], bank[7][0:HEADS, 0:TH], hcol[:, 0:1], None, ALU.add).then_inc(dt_v, 1)
            dve.wait_ge(dt_s, 1)
            dve.tensor_scalar(hcol[:, 3:4], hcol[:, 2:3], -1.0, None, ALU.mult).then_inc(dt_v, 1)
            dve.wait_ge(dt_s, 3)
            dve.tensor_scalar(dtw, dte_, 1.0, None, ALU.add).then_inc(dt_v, 1)
            dve.wait_ge(dt_v, 4)
            dve.tensor_scalar(dta, dtw, -1.0, None, ALU.add).then_inc(dt_v, 1)
            dve.wait_ge(dt_v, 5)
            dve.tensor_tensor(dte_, dte_, dta, ALU.subtract).then_inc(dt_v, 1)
            dve.reciprocal(dtT, dtw).then_inc(dt_v, 1)
            dve.wait_ge(dt_v, 7)
            dve.tensor_tensor(dte_, dte_, dtT, ALU.mult).then_inc(dt_v, 1)
            dve.wait_ge(dt_s, 4)
            dve.scalar_tensor_tensor(dtl, dtv, 0.0, dtl, ALU.max, ALU.add).then_inc(dt_v, 1)
            dve.wait_ge(dt_v, 9)
            dve.tensor_tensor(dtT, dtl, dte_, ALU.add).then_inc(dt_v, 1)
            dve.wait_ge(dt_v, 10)
            dve.tensor_scalar(dta, dtT, hcol[:, 3:4], None, ALU.mult).then_inc(dt_v, 1)
            dve.wait_ge(dt_v, 11)
            for c in range(NC):
                dve.tensor_tensor_scan(aT[:, c * Q:(c + 1) * Q], ones[0:HEADS, :], dta[:, c * Q:(c + 1) * Q], 0.0,
                                       ALU.mult, ALU.add).then_inc(dt_v, 1)
            dve.wait_ge(dt_v, 15)
            dve.tensor_copy(sm[:, 0:4], aT.rearrange("p (c l) -> p c l", l=Q)[:, :, Q - 1]).then_inc(dt_v, 1)
            dve.tensor_copy(sm[:, 4:4 + NB], dtT[:, SEQ:T]).then_inc(dt_v, 1)
            dve.wait_ge(sm_in, 16)
            dve.wait_ge(dt_s, 6)
            dve.tensor_tensor(dte[:, :, :], smbc[:, :, 0:4].rearrange("p h c -> p c h"), acol[:, :, :], ALU.subtract).then_inc(dt_v, 1)
            for half, lo in ((0, 0), (1, HD)):
                rows = slice(lo, lo + HD)
                by = smbc[rows, :, :].rearrange("p (j h) v -> p j h v", h=2)[:, :, half, :]
                dve.tensor_copy(dtch[rows, :, :], by[:, :, 4:4 + NB]).then_inc(dt_v, 1)
                dve.tensor_copy(dcch[rows, :, :], by[:, :, 4 + NB:4 + 2 * NB]).then_inc(dt_v, 1)
                dve.tensor_copy(dch[rows, :], dbc[rows, :].rearrange("p (j h) -> p j h", h=2)[:, :, half]).then_inc(dt_v, 1)
            dve.wait_ge(dt_v, 24)
            dve.wait_ge(dt_s, 9)

            with dve.Fori(0, GROUPS // 2) as G:
                for gg in range(2):
                    g = group_half(G, gg)

                    def conv(m, tile):
                        i = gg * 10 + m
                        e = CONVED.index(ORDER[m])
                        row = ext[:, e % 2, :]
                        dve.wait_ge(proj_free, G * 20 + (i + 3))
                        dve.wait_ge(silu_done, g * 6 + (e + 1))
                        dve.tensor_scalar(acc[:, :], row[:, 0:CONV0], cw0(0, tile), cb0(tile), ALU.mult, ALU.add).then_inc(tap, 1)
                        for k in range(1, TAPS0):
                            dve.wait_ge(tap, g * 18 + (3 * e + k))
                            t = dve.scalar_tensor_tensor(acc[:, :], row[:, k:k + CONV0], cw0(k, tile), acc[:, :], ALU.mult, ALU.add)
                            t.then_inc(tap if k < 3 else conv_done, 1)

                    def silu(e, dst):
                        dve.wait_ge(tanh_done, g * 6 + (e + 1))
                        dve.wait_ge(conv_done, g * 6 + (e + 1))
                        dve.scalar_tensor_tensor(dst, thx[:, :], 1.0, acc[:, :], ALU.add, ALU.mult).then_inc(silu_done, 1)

                    def weigh_dt(q):
                        dve.wait_ge(t_done, g * 4 + (q + 1))
                        scale = dtcol[:, :, ds(g * 8 + 2 * q, 2)].unsqueeze(3).broadcast_to([P, NC, 2, HD])
                        dve.tensor_tensor(xd[:, :, :].rearrange("p c (h d) -> p c h d", h=2),
                                          bank[4][:, :].rearrange("p (c h d) -> p c h d", c=NC, h=2), scale, ALU.mult).then_inc(xd_done, 1)

                    def causal(q):
                        dve.wait_ge(e_done, g * 4 + (q + 1))
                        if q == 0:
                            dve.wait_ge(cbm_done, g + 1)
                        cbm = CBm[:, :, :].rearrange("p c l -> p (c l)").unsqueeze(1).broadcast_to([P, 2, SEQ])
                        dve.tensor_tensor(em[:, :, :], em[:, :, :], cbm, ALU.mult).then_inc(m_done, 1)

                    def recur(q):
                        dve.wait_ge(s_done, g * 4 + (q + 1))
                        dve.tensor_copy(hs[:, 0, :], bank[5][:, 0:P]).then_inc(rec, 1)
                        for c in range(1, NC):
                            dve.wait_ge(rec, g * 28 + (7 * q + 2 * c - 1))
                            for h in range(2):
                                dve.scalar_tensor_tensor(hs[:, c, h * HD:(h + 1) * HD], hs[:, c - 1, h * HD:(h + 1) * HD],
                                                         cdbc[:, c, ds(g * 8 + (2 * q + h), 1)],
                                                         bank[5][:, c * P + h * HD:c * P + (h + 1) * HD],
                                                         ALU.mult, ALU.add).then_inc(rec, 1)

                    def skip(q):
                        dve.wait_ge(sd_done, g * 4 + (q + 2))
                        yt = ybuf[:, ds(g * 4 + q, 1), :].squeeze(1)
                        d = dch[:, ds(g * 4 + q, 1)]
                        dve.scalar_tensor_tensor(yt[:, 0:SEQ], xs[:, q % 2, 0:SEQ], d, bank[6][:, :], ALU.mult, ALU.add).then_inc(yd_done, 1)
                        dve.tensor_scalar(yt[:, SEQ:T], dec_conv(xs[:, q % 2, :]), d, None, ALU.mult).then_inc(yd_done, 1)

                    def add_earlier(q):
                        dve.wait_ge(o_done, g * 4 + (q + 1))
                        dve.wait_ge(ech_done, g * 4 + (q + 2))
                        dve.tensor_tensor(yob[:, :], bank[7][:, Q:SEQ], ech[:, Q:SEQ], ALU.mult).then_inc(yo_done, 1)
                        dve.wait_ge(yo_done, g * 4 + (q + 2))
                        dve.wait_ge(yd_done, g * 8 + (2 * q + 3))
                        yt = ybuf[:, ds(g * 4 + q, 1), :].squeeze(1)
                        dve.tensor_tensor(yt[:, Q:SEQ], yt[:, Q:SEQ], yob[:, :], ALU.add).then_inc(y_done, 1)

                    def sample_decay(q):
                        dve.tensor_tensor(dtx[:, :], dec_conv(xs[:, q % 2, :]), dtch[:, ds(g * 4 + q, 1), :].squeeze(1),
                                          ALU.mult).then_inc(dtx_done, 1)
                        dve.wait_ge(st_ld[q % 2], g * 32 + 16 * (q // 2 + 1))
                        s = st[:, q % 2, :].rearrange("p (b n) -> p b n", n=NS)
                        dve.tensor_tensor(s, s, dcch[:, ds(g * 4 + q, 1), :].squeeze(1).unsqueeze(2).broadcast_to([P, NB, NS]),
                                          ALU.mult).then_inc(dh_done, 1)

                    def sample_add(q):
                        dve.wait_ge(t1_done, g * 4 + (q + 1))
                        dve.wait_ge(dh_done, g * 4 + (q + 1))
                        dve.tensor_tensor(st[:, q % 2, :], st[:, q % 2, :], tdf, ALU.add).then_inc(st_new, 1)

                    def sample_out(q):
                        dve.wait_ge(t2_done, g * 4 + (q + 1))
                        dve.tensor_reduce(yr[:, :], tdec[:, :, :], AX, ALU.add).then_inc(yr_done, 1)
                        dve.wait_ge(yr_done, g * 4 + (q + 1))
                        yt = ybuf[:, ds(g * 4 + q, 1), :].squeeze(1)[:, SEQ:T]
                        dve.tensor_tensor(yt, yt, yr[:, :], ALU.add).then_inc(ydec_done, 1)

                    def silu_z(q):
                        dve.wait_ge(zt_done, g * 4 + (q + 1))
                        dve.scalar_tensor_tensor(zh[:, q % 2, :], th[:, :], 1.0, zh[:, q % 2, :], ALU.add, ALU.mult).then_inc(sz_done, 1)

                    conv(0, g + TILES)
                    silu(0, BT[:, :])
                    conv(1, g + (TILES + GROUPS))
                    silu(1, CT[:, :])
                    conv(2, g * 4)
                    silu(2, xs[:, 0, :])
                    dve.wait_ge(cb_done, g + 1)
                    dve.tensor_tensor(CBm[:, :, :], bank[5][:, :].rearrange("p (c l) -> p c l", l=Q),
                                      mask[:, :].unsqueeze(1).broadcast_to([P, NC, Q]), ALU.mult).then_inc(cbm_done, 1)
                    dve.wait_ge(bct_done, g + 1)
                    dve.wait_ge(bcd_out, g * 16 + 16)
                    dve.tensor_copy(bcd[:, :, :], bank[6][0:NB, 0:2 * NS].rearrange("b (a n) -> b a n", n=NS)).then_inc(bcd_done, 1)
                    causal(0)
                    weigh_dt(0)
                    conv(3, g * 4 + 1)
                    silu(3, xs[:, 1, :])
                    sample_decay(0)
                    silu_z(0)
                    recur(0)
                    skip(0)
                    conv(5, g * 4 + 2)
                    sample_add(0)
                    silu(4, xs[:, 0, :])
                    weigh_dt(1)
                    causal(1)
                    add_earlier(0)
                    sample_out(0)
                    sample_decay(1)
                    silu_z(1)
                    recur(1)
                    skip(1)
                    conv(7, g * 4 + 3)
                    sample_add(1)
                    silu(5, xs[:, 1, :])
                    weigh_dt(2)
                    causal(2)
                    add_earlier(1)
                    sample_out(1)
                    sample_decay(2)
                    silu_z(2)
                    recur(2)
                    skip(2)
                    weigh_dt(3)
                    sample_add(2)
                    causal(3)
                    silu_z(3)
                    add_earlier(2)
                    sample_out(2)
                    sample_decay(3)
                    recur(3)
                    skip(3)
                    add_earlier(3)
                    sample_add(3)
                    sample_out(3)

            for g in range(GROUPS):
                dve.wait_ge(rs_sqrt, g + 1)
                dve.reciprocal(sqs[:, g, :], sqs[:, g, :]).then_inc(rs_done, 1)

            def out_phase(base, layer):
                def scale(r):
                    dve.wait_ge(rs_done, r // STEPS + 1)
                    dve.wait_ge(gate_done, TILES)
                    dve.scalar_tensor_tensor(ybuf[:, r, :], ybuf[:, r, :], colB[:, ng + r:ng + r + 1], sqs[:, r // STEPS, :],
                                             ALU.mult, ALU.mult).then_inc(ys_done, 1)
                if layer == 0:
                    scale(0)
                for r in range(2 * TILES):
                    if layer == 0 and r + 1 < TILES:
                        scale(r + 1)
                    dve.wait_ge(y_hi, layer * 32 + r + 1)
                    if layer == 0 and r < TILES:
                        dve.wait_ge(ys_done, r + 1)
                    if layer == 1 and r < TILES:
                        dve.wait_ge(bg_free, r + 2)
                    dve.wait_ge(proj_done, base if r < 8 else base + (r - 8) // 2 + 1)
                    dve.tensor_tensor(hlo[:, r % 8, :], ybuf[:, r % TILES, :], hhi[:, r % 8, :].bitcast(F32), ALU.subtract).then_inc(y_lo, 1)
                    if r == TILES + 7:
                        residual(base, layer, 0)
                residual(base, layer, 1)

            def residual(base, layer, half):
                for i in range(4):
                    if i < 3:
                        dve.wait_ge(out_mm, 6 * layer + 3 * half + i + 1)
                    else:
                        dve.wait_ge(proj_done, base + 8 * (half + 1))
                    k = 4 * half + i
                    dve.tensor_tensor(xT[:, k, 0:TH], xT[:, k, 0:TH], bank[2 * i][:, 0:TH], ALU.add)
                    dve.tensor_tensor(xT[:, k, TH:T], xT[:, k, TH:T], bank[2 * i + 1][:, 0:TH], ALU.add).then_inc(out_evac, 1)

            out_phase(OUT0, 0)

            for k in range(KT):
                dve.wait_ge(h_hi, KT + k + 1)
                dve.wait_ge(out_evac, 4 + k + 1)
                dve.scalar_tensor_tensor(hlo[:, k, :], xT[:, k, :], colB[:, n1 + k:n1 + k + 1], hhi[:, k, :].bitcast(F32),
                                         ALU.mult, ALU.subtract).then_inc(h_lo, 1)
            r1, r2 = sqs[:, 1, :], sqs[:, 2, :]
            dve.wait_ge(rs_sqrt, GROUPS + 1)
            dve.reciprocal(r1, r1).then_inc(rs_done, 1)
            dve.wait_ge(rs_done, GROUPS + 1)
            dve.tensor_tensor(r2, r1, r1, ALU.mult).then_inc(rs_done, 1)
            dve.wait_ge(rs_done, GROUPS + 2)

            dve.memset(ext[:, :, 0:PRE1], 0.0).then_inc(cs1_done, 1)
            with dve.Fori(0, TILES // 2) as J:
                for jj in range(2):
                    j = J * 2 + jj
                    row = ext[:, jj, 0:EXT1]
                    dec = row[:, DEC1:EXT1].rearrange("p (b k) -> p b k", k=TAPS1)
                    u, zr, cv, c2 = zh[:, 0, :], zh[:, 1, :], acc[:, 0:CONV1], thx[:, 0:T]
                    dve.wait_ge(proj_done, j * 4 + (IN1 + 1))
                    dve.tensor_tensor(u[:, 0:TH], bank[0][:, 0:TH], r2[:, 0:TH], ALU.mult).then_inc(u_done, 1)
                    dve.tensor_tensor(u[:, TH:T], bank[1][:, 0:TH], r2[:, TH:T], ALU.mult).then_inc(cg_free, 1)
                    dve.tensor_copy(dec[:, :, 0:PRE1], cst1[:, ds(j, 1), :, :].squeeze(1)).then_inc(cs1_done, 1)
                    dve.wait_ge(proj_done, j * 4 + (IN1 + 2))
                    dve.wait_ge(cg_free, j + 2)
                    dve.tensor_tensor(row[:, PRE1:PRE1 + TH], bank[2][:, 0:TH], u[:, 0:TH], ALU.mult)
                    dve.tensor_tensor(row[:, PRE1 + TH:PRE1 + SEQ], bank[3][:, 0:SEQ - TH], u[:, TH:SEQ], ALU.mult)
                    dve.tensor_tensor(dec[:, :, PRE1], bank[3][:, SEQ - TH:TH], u[:, SEQ:T], ALU.mult).then_inc(xin_free, 1)
                    dve.wait_ge(xin_free, j + 2)
                    dve.tensor_scalar(cv, row[:, 0:CONV1], colB[:, ds(j + c1, 1)], None, ALU.mult).then_inc(tap1, 1)
                    dve.tensor_copy(tail1[:, 0:PRE1, ds(j, 1)].squeeze(2), row[:, SEQ:SEQ + PRE1])
                    dve.tensor_copy(tail1[:, PRE1:TAIL1, ds(j, 1)].squeeze(2), dec[:, :, PRE1]).then_inc(tail1_done, 1)
                    for k in range(1, TAPS1):
                        dve.wait_ge(tap1, j * 3 + k)
                        dve.scalar_tensor_tensor(cv, row[:, k:k + CONV1], colB[:, ds(j + (c1 + k * TILES), 1)], cv,
                                                 ALU.mult, ALU.add).then_inc(tap1, 1)
                    dve.wait_ge(proj_done, j * 4 + (IN1 + 4))
                    dve.tensor_tensor(zr[:, 0:TH], bank[6][:, 0:TH], r1[:, 0:TH], ALU.mult)
                    dve.tensor_tensor(zr[:, TH:T], bank[7][:, 0:TH], r1[:, TH:T], ALU.mult).then_inc(z_free, 1)
                    dve.wait_ge(sl_done, j + 1)
                    dve.tensor_tensor(c2, th[:, :], r1, ALU.mult).then_inc(slr_done, 1)
                    dve.wait_ge(tap1, j * 3 + 3)
                    dve.wait_ge(slr_done, j + 2)
                    dve.tensor_tensor(c2[:, 0:SEQ], c2[:, 0:SEQ], cv[:, 0:SEQ], ALU.mult)
                    dve.tensor_tensor(c2[:, SEQ:T], c2[:, SEQ:T],
                                      cv[:, DEC1:CONV1:TAPS1],
                                      ALU.mult).then_inc(c2_done, 1)
                    dve.wait_ge(c2_done, j + 1)
                    yt = ybuf[:, ds(j, 1), :].squeeze(1)
                    dve.tensor_tensor(yt[:, 0:TH], bank[4][:, 0:TH], c2[:, 0:TH], ALU.mult)
                    dve.tensor_tensor(yt[:, TH:T], bank[5][:, 0:TH], c2[:, TH:T], ALU.mult).then_inc(bg_free, 1)

            out_phase(OUT1, 1)

            for k in range(KT):
                dve.wait_ge(sq_done, TILES + KT + k + 1)
                if k == 0:
                    dve.tensor_copy(sqs[:, 0, :], sqb[:, :]).then_inc(ydec_done, 1)
                else:
                    dve.wait_ge(ydec_done, TILES + k)
                    dve.tensor_tensor(sqs[:, 0, :], sqs[:, 0, :], sqb[:, :], ALU.add).then_inc(ydec_done, 1)
            dve.wait_ge(col_rms, 1)
            dve.reciprocal(ssq[:, 0:4], ssq[:, 0:4])
            dve.reciprocal(ssq[0:NB, 4:5], ssq[0:NB, 4:5]).then_inc(col_rcp, 1)
            dve.wait_ge(col_rcp, 1)
            for t in range(5):
                rows = P if t < 4 else NB
                dve.wait_ge(fin_tr, t + 1)
                dve.tensor_scalar(x_nat[t][:, 512:D], bank[(2 * t + 1) % 8][0:rows, :], ssq[0:rows, t:t + 1], None,
                                  ALU.mult).then_inc(evac_a, 1)

        @block.tensor
        def _(pe):
            pe.sem_inc(sd_done, 1)

            def transpose(dst, src):
                n = src.shape[0]
                return pe.matmul(dst, src, ident[0:n, 0:n], is_transpose=True, start=True, stop=True)

            pe.wait_ge(consts, 8)
            pe.wait_ge(par_in, 160)
            transpose(bank[7][:, 0:P], rowsA[:, :])
            transpose(bank[7][:, P:P + 80], rowsB[:, :]).then_inc(par_t, 1)
            for t in range(5):
                pe.wait_ge(x_in[t], 16)
            for k in range(KT):
                if k >= 4:
                    pe.wait_ge(xt_out, k - 3)
                for t in range(4):
                    mm = transpose(bank[k % 4][:, t * P:(t + 1) * P], x_nat[t][:, k * P:(k + 1) * P])
                mm.then_inc(xt_done, 1)
            for k in range(KT):
                mm = transpose(bank[4][:, k * NB:(k + 1) * NB], x_nat[4][:, k * P:(k + 1) * P])
            mm.then_inc(xt_done, 1)
            pe.wait_ge(diag_done, 5)
            for t in range(4):
                pe.matmul(bank[5][:, t * P:(t + 1) * P], ones[:, :], xdd[:, t, :], start=True, stop=True)
            pe.matmul(bank[6][:, 0:NB], ones[0:NB, :], finb[0:NB, 0:NB], start=True, stop=True).then_inc(rb_done, 1)
            pe.wait_ge(cs_in, 32)
            pe.wait_ge(xt_out, KT)
            for t in range(CT_TILES):
                mm = transpose(bank[t // 12][:, t % 12 * 24:(t % 12 + 1) * 24], cs_nat[:, t * P:(t + 1) * P])
                if t % 12 == 11:
                    mm.then_inc(cs_t, 1)
            for t in range(TILES):
                mm = transpose(bank[2][:, t * 16:(t + 1) * 16], ss_nat[:, t * P:(t + 1) * P])
            mm.then_inc(cs_t, 1)

            pe.wait_ge(dtw_hi, 1)
            pe.wait_ge(dtw_lo, 1)
            pe.wait_ge(rb_out, 1)
            pe.wait_ge(par_c, 1)
            for k in range(KT):
                pe.wait_ge(h_hi, k + 1)
                pe.wait_ge(h_lo, k + 1)
                for i, (w, h) in enumerate(((dwh, hhi), (dwh, hlo), (dwl, hhi))):
                    for half in range(2):
                        mm = pe.matmul(bank[6 + half][0:HEADS, 0:TH], w[:, k, :], h[:, k, half * TH:(half + 1) * TH],
                                       start=(k == 0 and i == 0), stop=(k == KT - 1 and i == 2))
            mm.then_inc(dt_mm, 1)

            def project(n, slot, b0, b1):
                pe.wait_ge(hi_done, n + (SLOT + 1))
                pe.wait_ge(lo_done, n + (SLOT + 1))
                for k in range(KT):
                    for i, (w, h) in enumerate(((whi, hhi), (whi, hlo), (wlo, hhi))):
                        for b, cols in ((b0, slice(0, TH)), (b1, slice(TH, T))):
                            mm = pe.matmul(b[:, 0:TH], w[:, slot, k * P:(k + 1) * P], h[:, k, cols],
                                           start=(k == 0 and i == 0), stop=(k == KT - 1 and i == 2))
                mm.then_inc(proj_done, 1)

            def columns():
                pe.wait_ge(dt_v, 17)
                for c in range(NC):
                    transpose(bank[7][:, c * HEADS:(c + 1) * HEADS], aT[:, c * Q:(c + 1) * Q])
                for c in range(NC):
                    mm = transpose(bank[7][:, P + c * HEADS:P + (c + 1) * HEADS], dtT[:, c * Q:(c + 1) * Q])
                mm.then_inc(col_t, 1)

            columns()
            with pe.Fori(0, GROUPS // 2) as G:
                for gg in range(2):
                    g = group_half(G, gg)

                    def proj(m):
                        i = gg * 10 + m
                        pe.wait_ge(proj_free, G * 20 + (i + 1))
                        if m == 0 and gg == 0:
                            pe.wait_ge(cs_c, 3)
                        project(G * 20 + i, i % SLOT, bank[2 * (m % 2)], bank[2 * (m % 2) + 1])

                    def group_matrices():
                        pe.wait_ge(silu_done, g * 6 + 3)
                        for c in range(NC):
                            mm = transpose(bank[4][:, c * Q:(c + 1) * Q], BT[:, c * Q:(c + 1) * Q])
                        mm.then_inc(tb_done, 1)
                        pe.wait_ge(fin_done, g * 4 + 1)
                        for c in range(NC):
                            mm = pe.matmul(bank[5][:, c * Q:(c + 1) * Q], BT[:, c * Q:(c + 1) * Q], CT[:, c * Q:(c + 1) * Q],
                                           start=True, stop=True)
                        mm.then_inc(cb_done, 1)
                        pe.wait_ge(yd_done, g * 8 + 1)
                        transpose(bank[6][0:NB, 0:NS], dec_conv(BT))
                        transpose(bank[6][0:NB, NS:2 * NS], dec_conv(CT)).then_inc(bct_done, 1)

                    def turn(q):
                        pe.wait_ge(silu_done, g * 6 + (q + 4))
                        if q == 0:
                            pe.wait_ge(bs_done, g + 1)
                        for c in range(NC):
                            mm = transpose(bank[4][:, c * Q:(c + 1) * Q], xs[:, q % 2, c * Q:(c + 1) * Q])
                        mm.then_inc(t_done, 1)

                    def within(q):
                        pe.wait_ge(xdd_done, g * 4 + (q + 1))
                        pe.wait_ge(fin_done, g * 4 + (q + 1))
                        if q == 0:
                            pe.wait_ge(cbm_done, g + 1)
                        for c in range(NC):
                            mm = pe.matmul(bank[5][:, c * P:(c + 1) * P], Bs[:, c, :], xdd[:, c, :], start=True, stop=True)
                        mm.then_inc(s_done, 1)
                        pe.wait_ge(m_done, g * 4 + (q + 1))
                        if q == 0:
                            pe.wait_ge(bcd_done, g + 1)
                        else:
                            pe.wait_ge(yd_done, g * 8 + 2 * q)
                        for c in range(NC):
                            for h in range(2):
                                mm = pe.matmul(bank[6][h * HD:(h + 1) * HD, c * Q:(c + 1) * Q], xd[:, c, h * HD:(h + 1) * HD],
                                               em[:, h, c * Q:(c + 1) * Q], start=True, stop=True)
                        mm.then_inc(sd_done, 1)

                    def across(q):
                        pe.wait_ge(rec, g * 28 + 7 * (q + 1))
                        transpose(bank[5][:, 0:NS], hs[:, NC - 1, :]).then_inc(fin_t, 1)
                        pe.wait_ge(yo_done, g * 4 + (q + 1))
                        for c in range(1, NC):
                            mm = pe.matmul(bank[7][:, c * Q:(c + 1) * Q], hs[:, c - 1, :], CT[:, c * Q:(c + 1) * Q],
                                           start=True, stop=True)
                        mm.then_inc(o_done, 1)

                    proj(0)
                    proj(1)
                    proj(2)
                    group_matrices()
                    proj(3)
                    turn(0)
                    proj(4)
                    within(0)
                    proj(5)
                    across(0)
                    turn(1)
                    proj(6)
                    within(1)
                    proj(7)
                    across(1)
                    turn(2)
                    proj(8)
                    within(2)
                    turn(3)
                    proj(9)
                    across(2)
                    within(3)
                    across(3)

            pe.wait_ge(proj_free, OUT0 + 2)
            tf = tail0[:, :, :].rearrange("p r t -> p (r t)")
            for i in range(3):
                n = 96 if i < 2 else 72
                mm = transpose(bank[0][0:n, i * P:(i + 1) * P], tf[:, i * 96:i * 96 + n])
            mm.then_inc(tail_t, 1)
            pe.wait_ge(ydec_done, TILES)
            pe.wait_ge(fin_done, TILES + 1)
            for g in range(GROUPS):
                pe.wait_ge(sqs_done, STEPS * (g + 1) + 1)
                if g == 3:
                    pe.wait_ge(tail_c, 1)
                for half, b in enumerate((bank[(2 * g + 2) % 8], bank[(2 * g + 3) % 8])):
                    mm = pe.matmul(b[:, 0:TH], ones[:, :], sqs[:, g, half * TH:(half + 1) * TH], start=True, stop=True)
                mm.then_inc(stat_mm, 1)

            def out_phase(base, layer):
                with pe.Fori(0, 2) as half:
                    for c in range(8):
                        pe.wait_ge(hi_done, half * 8 + (base + c + SLOT + 1))
                        pe.wait_ge(lo_done, half * 8 + (base + c + SLOT + 1))
                        pe.wait_ge(y_hi, half * 16 + (32 * layer + 2 * c + 2))
                        pe.wait_ge(y_lo, half * 16 + (32 * layer + 2 * c + 2))
                        for i in range(4):
                            if c == 0:
                                pe.wait_ge(out_evac, half * 4 + (8 * layer + i + 1))
                            for kk in range(2):
                                r = (2 * c + kk) % 8
                                for v, (w, h) in enumerate(((whi, hhi), (whi, hlo), (wlo, hhi))):
                                    for hb in range(2):
                                        mm = pe.matmul(bank[2 * i + hb][:, 0:TH],
                                                       w[:, c % SLOT, kk * 512 + i * P:kk * 512 + (i + 1) * P],
                                                       h[:, r, hb * TH:(hb + 1) * TH],
                                                       start=(c == 0 and kk == 0 and v == 0),
                                                       stop=(c == 7 and kk == 1 and v == 2))
                            if c == 7 and i < 3:
                                mm.then_inc(out_mm, 1)
                        mm.then_inc(proj_done, 1)

            pe.wait_ge(rs_done, GROUPS)
            out_phase(OUT0, 0)

            def block1(j, first=False):
                def part(m):
                    project(j * 4 + (IN1 + m), m, bank[2 * m], bank[2 * m + 1])
                pe.wait_ge(cg_free, j + 1)
                part(0)
                pe.wait_ge(xin_free, j + 1)
                part(1)
                pe.wait_ge(bg_free, j + 1)
                part(2)
                if first:
                    pe.wait_ge(sqs_done, TILES + KT + 1)
                    for half in range(2):
                        mm = pe.matmul(bank[6 + half][:, 0:TH], ones[:, :], sqs[:, 0, half * TH:(half + 1) * TH], start=True, stop=True)
                    mm.then_inc(stat_mm, 1)
                    pe.wait_ge(rs_sqrt, GROUPS + 1)
                pe.wait_ge(z_free, j + 1)
                part(3)

            for k in range(KT):
                pe.wait_ge(h_hi, KT + k + 1)
                pe.wait_ge(h_lo, KT + k + 1)
            block1(0, first=True)
            with pe.Fori(1, TILES) as j:
                block1(j)

            pe.wait_ge(tail1_done, TILES)
            pe.wait_ge(cg_free, TILES + 1)
            tf1 = tail1[:, :, :].rearrange("p r t -> p (r t)")
            for i in range(2):
                mm = transpose(bank[0][0:80, i * P:(i + 1) * P], tf1[:, i * 80:(i + 1) * 80])
            mm.then_inc(tail_t, 1)
            pe.wait_ge(tail_c, 2)
            pe.wait_ge(bg_free, TILES + 1)
            out_phase(OUT1, 1)

            pe.wait_ge(wf_done, KT)
            def back(t):
                for k in range(KT):
                    rows, cols = (P, slice(t * P, (t + 1) * P)) if t < 4 else (NB, slice(SEQ, T))
                    mm = transpose(bank[(2 * t + k // 4) % 8][0:rows, k % 4 * P:(k % 4 + 1) * P], xT[:, k, cols])
                mm.then_inc(fin_tr, 1)
            for t in range(3):
                back(t)
            pe.wait_ge(ydec_done, TILES + KT)
            for t in range(5):
                rows, cols = (P, slice(t * P, (t + 1) * P)) if t < 4 else (NB, slice(SEQ, T))
                mm = pe.matmul(bank[7][0:rows, t:t + 1], sqs[:, 0, cols], ones[:, 0:1], start=True, stop=True)
            mm.then_inc(col_sq, 1)
            pe.wait_ge(col_rms, 1)
            back(3)
            pe.wait_ge(fin_ev, 1)
            pe.wait_ge(evac_a, 1)
            back(4)


_INS = ["x_prompt", "x_sample", "state_ssm", "state_ssm_conv", "state_sconv", "norm_w", "final_norm_w", "ssd_w_in",
        "ssd_conv_w", "ssd_conv_b", "ssd_dt_bias", "ssd_A_log", "ssd_D", "ssd_norm_w", "ssd_w_out", "sc_w_in",
        "sc_conv_w", "sc_w_out"]
_OUTS = {"y_prompt": (1, SEQ, D), "y_sample": (NB, 1, D), "new_ssm_p": (1, 1, HEADS, HD, NS),
         "new_ssm_conv_p": (1, 1, PRE0, XBC), "new_sconv_p": (1, 1, PRE1, DI), "new_ssm_s": (1, NB, HEADS, HD, NS),
         "new_ssm_conv_s": (1, NB, PRE0, XBC), "new_sconv_s": (1, NB, PRE1, DI)}


def kernel(**inputs):
    import numpy as np
    import concourse.bacc as bacc
    from concourse.bass_utils import run_bass_kernel_spmd

    nc = bacc.Bacc("TRN2", target_bir_lowering=False, num_devices=1)
    arrays = {f"in_{n}": np.ascontiguousarray(inputs[n]) for n in _INS}
    ins = {n: nc.dram_tensor(f"in_{n}", arrays[f"in_{n}"].shape, F32, kind="ExternalInput").ap() for n in _INS}
    outs = {n: nc.dram_tensor(f"out_{n}", s, F32, kind="ExternalOutput").ap() for n, s in _OUTS.items()}
    hybrid_step(nc, ins, outs)
    r = run_bass_kernel_spmd(nc, [arrays], core_ids=[0])
    return tuple(r.results[0][f"out_{n}"] for n in _OUTS)
```

```python
from contextlib import ExitStack

import concourse.bass as bass
from concourse import mybir

F32 = mybir.dt.float32
F32R = mybir.dt.float32r
ALU = mybir.AluOpType
ACT = mybir.ActivationFunctionType
AX = mybir.AxisListType.X
ds = bass.ds

P = 128
D = 1024
SEQ = 512
NB = 8
T = SEQ + NB
TH = T // 2
KT = D // P
DI = 2048
HEADS, HD, GROUPS, NS = 32, 64, 4, 128
Q = 128
NC = SEQ // Q
XBC = DI + 2 * GROUPS * NS
TILES = DI // P
STEPS = TILES // GROUPS
CT_TILES = XBC // P
EPS = 1e-5

TAPS0, TAPS1 = 4, 3
RAW, SLOT = 2, 4
PRE0, PRE1 = TAPS0 - 1, TAPS1 - 1
EXT0 = PRE0 + SEQ + NB * TAPS0
EXT1 = PRE1 + SEQ + NB * TAPS1
CONV0, CONV1 = EXT0 - PRE0, EXT1 - PRE1
DEC0, DEC1 = PRE0 + SEQ, PRE1 + SEQ
TAIL0, TAIL1 = PRE0 + NB, PRE1 + NB

ORDER = ["B", "C", "x0", "x1", "x2", "x3", "z0", "z1", "z2", "z3"]
CONVED = ["B", "C", "x0", "x1", "x2", "x3"]
OUT0 = len(ORDER) * GROUPS
IN1 = OUT0 + 16
OUT1 = IN1 + 4 * TILES
CHUNKS = OUT1 + 16


def hybrid_step(nc, ins, outs):
    x_prompt, x_sample = ins["x_prompt"], ins["x_sample"]

    with ExitStack() as ctx:
        def sb(name, shape, dt=F32):
            return ctx.enter_context(nc.sbuf_tensor(name, shape, dt))

        def sem(name):
            return ctx.enter_context(nc.semaphore(name))

        bank = [ctx.enter_context(nc.psum_tensor(f"bank{i}", [P, 512], F32)) for i in range(8)]

        xT = sb("xT", [P, KT, T])
        hhi = sb("hhi", [P, KT, T], F32R)
        hlo = sb("hlo", [P, KT, T], F32R)
        raw = sb("raw", [P, RAW, 1024])
        whi = sb("whi", [P, SLOT, 1024], F32R)
        wlo = sb("wlo", [P, SLOT, 1024], F32R)
        ybuf = sb("ybuf", [P, TILES, T])
        ext = sb("ext", [P, 2, EXT0])
        acc = sb("acc", [P, CONV0])
        thx = sb("thx", [P, CONV0])
        xs = sb("xs", [P, 2, CONV0])
        BT = sb("BT", [P, CONV0])
        CT = sb("CT", [P, CONV0])
        Bs = sb("Bs", [P, NC, NS])
        CBm = sb("CBm", [P, NC, Q])
        xd = sb("xd", [P, NC, P])
        xdd = sb("xdd", [P, NC, P])
        abc = sb("abc", [P, 2, SEQ])
        em = sb("em", [P, 2, SEQ])
        ech = sb("ech", [P, SEQ])
        hs = sb("hs", [P, NC, P])
        yob = sb("yob", [P, SEQ - Q])
        finb = sb("finb", [P, NS])
        st = sb("st", [P, 2, NB * NS])
        tdec = sb("tdec", [P, NB, NS])
        bcbc = sb("bcbc", [P, NB, 2, NS])
        bcd = sb("bcd", [NB, 2, NS])
        dtx = sb("dtx", [P, 2, NB])
        yr = sb("yr", [P, NB])
        zh = sb("zh", [P, 2, T])
        th = sb("th", [P, T])
        sqb = sb("sqb", [P, T])
        sqs = sb("sqs", [P, GROUPS, T])
        ident = sb("ident", [P, P])
        mask = sb("mask", [P, Q])
        ones = sb("ones", [P, P])
        colA = sb("colA", [P, P])
        colB = sb("colB", [P, 80])
        cst0 = sb("cst0", [P, CT_TILES, NB, PRE0])
        cst1 = sb("cst1", [P, TILES, NB, PRE1])
        tail0 = sb("tail0", [P, TAIL0, CT_TILES])
        dbc = sb("dbc", [P, HEADS])
        dch = sb("dch", [P, TILES])
        hcol = sb("hcol", [HEADS, 4])
        sm = sb("sm", [HEADS, 4 + 2 * NB])
        acol = sb("acol", [P, NC, HEADS])
        dtcol = sb("dtcol", [P, NC, HEADS])
        dte = sb("dte", [P, NC, HEADS])
        cdbc = sb("cdbc", [P, NC, HEADS])
        dtch = sb("dtch", [P, TILES, NB])
        dcch = sb("dcch", [P, TILES, NB])
        ssq = sb("ssq", [P, 8])
        eps = sb("eps", [P, 1])

        flat = ybuf[:, :, :].rearrange("p a b -> p (a b)")
        x_nat = [flat[:, t * D:(t + 1) * D] for t in range(4)] + [flat[0:NB, 4 * D:5 * D]]
        cs_nat = flat[0:NB * PRE0, 5 * D:5 * D + XBC]
        ss_nat = st[0:NB * PRE1, :, :].rearrange("p a b -> p (a b)")
        htmp = [acc[:, 0:T], thx[:, 0:T], xs[:, 0, 0:T], xs[:, 1, 0:T]]
        emf = em[:, :, :].rearrange("p a b -> p (a b)")
        tdf = tdec[:, :, :].rearrange("p a b -> p (a b)")
        bcf = bcbc[:, :, :, :].rearrange("p a b c -> p (a b c)")
        dtv, dta, dte_, dtw = (bcf[0:HEADS, 0:T], bcf[0:HEADS, T:2 * T], bcf[0:HEADS, 2 * T:3 * T],
                               tdf[0:HEADS, 0:T])
        dtl, dtT, aT = zh[0:HEADS, 0, :], zh[0:HEADS, 1, :], th[0:HEADS, 0:SEQ]
        sqj = emf[:, 0:D]
        xdf = xd[:, :, :].rearrange("p a b -> p (a b)")
        rowsA, rowsB = xdf[:, 0:P], xdf[0:80, P:2 * P]
        dwr = abc[:, 0, 0:KT * HEADS].rearrange("p (k h) -> p k h", h=HEADS)
        dwh, dwl = (w[:, SLOT - 1, 0:KT * HEADS].rearrange("p (k h) -> p k h", h=HEADS) for w in (whi, wlo))
        SMN = NC + 2 * NB
        smd = emf[0:HEADS, 0:HEADS * SMN].rearrange("p (v h) -> p v h", h=HEADS)
        tb0 = emf[0:96, 0:3 * P].rearrange("p (i c) -> p i c", c=P)
        tb1 = emf[0:80, 3 * P:5 * P].rearrange("p (i c) -> p i c", c=P)
        tail1 = cst0[:, :, :, :].rearrange("p t b k -> p (t b k)")[:, 0:TAIL1 * TILES].rearrange("p (r t) -> p r t", t=TILES)
        rb0 = sqb
        dcf = dcch[:, :, :].rearrange("p t b -> p (t b)")

        def cw0(k, t):
            return colA[:, ds(k * CT_TILES + t, 1)]

        def cb0(t):
            return colA[:, ds(TAPS0 * CT_TILES + t, 1)]
        n0 = TAPS0 * CT_TILES + CT_TILES
        n1, nf, ng, c1 = 0, KT, 2 * KT, 2 * KT + TILES

        stat_banks = [(bank[a], bank[b]) for a, b in ((4, 5), (0, 1), (2, 3), (6, 7))]

        a_dram = nc.dram_tensor("a_rows", [HEADS, SEQ], F32, kind="Internal").ap()
        bc_dram = nc.dram_tensor("bc_rows", [GROUPS, NB, 2 * NS], F32, kind="Internal").ap()

        w_in0 = ins["ssd_w_in"][0].rearrange("(k p) n -> p k n", p=P)
        w_out0 = ins["ssd_w_out"][0].rearrange("(k p) n -> p k n", p=P)
        w_in1 = ins["sc_w_in"][0].rearrange("(k p) n -> p k n", p=P)
        w_out1 = ins["sc_w_out"][0].rearrange("(k p) n -> p k n", p=P)
        st_in = ins["state_ssm"][0].rearrange("b h p n -> (h p) b n")
        st_out = outs["new_ssm_s"][0].rearrange("b h p n -> (h p) b n")
        fin_out = outs["new_ssm_p"][0, 0].rearrange("h p n -> (h p) n")

        x_in = [sem(f"x_in{t}") for t in range(5)]
        par_in = sem("par_in")
        cs_in = sem("cs_in")
        dtw_in = sem("dtw_in")
        raw_in = [sem(f"raw_in{s}") for s in range(SLOT)]
        hi_done = sem("hi_done")
        lo_done = sem("lo_done")
        proj_done = sem("proj_done")
        proj_free = sem("proj_free")
        consts = sem("consts")
        sqs_zero = sem("sqs_zero")
        par_t, par_c = sem("par_t"), sem("par_c")
        ssq_done, rms_done, ln_done, diag_done = (sem(n) for n in ("ssq_done", "rms_done", "ln_done", "diag_done"))
        xt_done, xt_out = sem("xt_done"), sem("xt_out")
        rb_done, rb_out = sem("rb_done"), sem("rb_out")
        cs_t, cs_c = sem("cs_t"), sem("cs_c")
        h_full, h_hi, h_lo, h_lo_p = sem("h_full"), sem("h_hi"), sem("h_lo"), sem("h_lo_p")
        dtw_hi, dtw_lo, dt_mm = sem("dtw_hi"), sem("dtw_lo"), sem("dt_mm")
        dt_v, dt_s = sem("dt_v"), sem("dt_s")
        a_out, smd_done, smb_done = sem("a_out"), sem("smd_done"), sem("smb_done")
        col_t = sem("col_t")
        tap0_done = sem("tap0_done")
        tap, conv_done, tanh_done, silu_done = sem("tap"), sem("conv_done"), sem("tanh_done"), sem("silu_done")
        tb_done, bs_done, cb_done, cbm_done = sem("tb_done"), sem("bs_done"), sem("cb_done"), sem("cbm_done")
        bct_done, bcd_done, bcd_out, bcbc_in = sem("bct_done"), sem("bcd_done"), sem("bcd_out"), sem("bcbc_in")
        t_done, xd_done, xdd_done = sem("t_done"), sem("xd_done"), sem("xdd_done")
        seg_done = sem("seg_done")
        abc_in, e_done, ech_done, m_done = sem("abc_in"), sem("e_done"), sem("ech_done"), sem("m_done")
        s_done, sd_done, rec, o_done = sem("s_done"), sem("sd_done"), sem("rec"), sem("o_done")
        fin_done, fin_st = sem("fin_done"), sem("fin_st")
        yd_done, yo_done, y_done = sem("yd_done"), sem("yo_done"), sem("y_done")
        st_ld, st_st = [sem(f"st_ld{s}") for s in range(2)], [sem(f"st_st{s}") for s in range(2)]
        dtx_done, t1_done, dh_done, st_new, t2_done = (sem(n) for n in ("dtx_done", "t1_done", "dh_done", "st_new", "t2_done"))
        yr_done, ydec_done = sem("yr_done"), sem("ydec_done")
        zt_done, sz_done, gate_done, sq_done, sqp_done, sqs_done = (sem(n) for n in ("zt_done", "sz_done", "gate_done", "sq_done", "sqp_done", "sqs_done"))
        tail_t, tail_c, tail_st = sem("tail_t"), sem("tail_c"), sem("tail_st")
        stat_mm, rs_done, r2_done, xsum_done, ys_done = (sem(n) for n in ("stat_mm", "rs_done", "r2_done", "xsum_done", "ys_done"))
        y_hi, y_lo = sem("y_hi"), sem("y_lo")
        out_mm, out_evac, evac_a = sem("out_mm"), sem("out_evac"), sem("evac_a")
        u_done, cg_free, xin_free, z_free, bg_free = (sem(n) for n in ("u_done", "cg_free", "xin_free", "z_free", "bg_free"))
        cs1_done, tail1_done, tap1, sl_done, slr_done, c2_done = (sem(n) for n in ("cs1_done", "tail1_done", "tap1", "sl_done", "slr_done", "c2_done"))
        wf_done, fin_tr, fin_ev, col_sq, col_rms, y_st = (sem(n) for n in ("wf_done", "fin_tr", "fin_ev", "col_sq", "col_rms", "y_st"))
        direct_st = sem("direct_st")

        turnstile, turnstile_p = sem("turnstile"), sem("turnstile_p")

        block = ctx.enter_context(nc.Block())

        def dec4(row):
            return row[:, DEC0:DEC0 + NB * TAPS0].rearrange("p (b k) -> p b k", k=TAPS0)

        def dec_conv(row):
            return row[:, DEC0:CONV0:TAPS0]

        def group_half(G, gg):
            return 2 * G + gg

        @block.sync
        def _(sp):
            def load(n, i, src):
                slot = i % RAW
                count = sp.snap(n + (1 + SLOT - RAW))
                sp.wait_ge(hi_done, count)
                sp.sem_inc(turnstile, 1)
                sp.wait_ge(lo_done, count)
                sp.sem_inc(turnstile, 1)
                k = src.shape[1]
                sp.dma_start(raw[:, slot, :].rearrange("p (k n) -> p k n", k=k), src).then_inc(raw_in[slot], 16)

            for t in range(4):
                sp.dma_start(x_nat[t], x_prompt[0, t * P:(t + 1) * P, :]).then_inc(x_in[t], 16)
            sp.dma_start(dwr[:, :, :], w_in0[:, :, DI + XBC:DI + XBC + HEADS]).then_inc(dtw_in, 16)
            with sp.Fori(0, GROUPS // 2) as G:
                for gg in range(2):
                    g = group_half(G, gg)
                    for m, what in enumerate(ORDER):
                        if what == "B":
                            col = g * NS + 2 * DI
                        elif what == "C":
                            col = g * NS + (2 * DI + GROUPS * NS)
                        else:
                            col = g * (STEPS * P) + (int(what[1]) * P + (DI if what[0] == "x" else 0))
                        i = gg * 10 + m
                        load(G * 20 + i, i, w_in0[:, :, ds(sp.snap(col), P)])

            def load_out(base, w):
                with sp.Fori(0, 2) as half:
                    for c in range(8):
                        load(half * 8 + (base + c), c, w[:, 2 * c:2 * c + 2, ds(sp.snap(half * 512), 512)])

            load_out(OUT0, w_out0)
            with sp.Fori(0, TILES) as j:
                for m, part in enumerate((3, 1, 2, 0)):
                    load(j * 4 + (IN1 + m), m, w_in1[:, :, ds(sp.snap(j * P + part * DI), P)])
            load_out(OUT1, w_out1)

            sp.dma_start(outs["new_ssm_conv_s"][0, :, 0:PRE0 - 1, :], ins["state_ssm_conv"][0, :, 1:PRE0, :]).then_inc(direct_st, 16)
            sp.dma_start(outs["new_sconv_s"][0, :, 0:PRE1 - 1, :], ins["state_sconv"][0, :, 1:PRE1, :]).then_inc(direct_st, 16)

            sp.wait_ge(tail_c, 1)
            cp = outs["new_ssm_conv_p"][0, 0].rearrange("r (t c) -> (r t) c", c=P)
            csv = outs["new_ssm_conv_s"][0, :, PRE0 - 1, :].rearrange("b (t c) -> b t c", c=P)
            sp.dma_start(cp, tb0[0:72, 0, :]).then_inc(tail_st, 16)
            sp.dma_start(csv[0], tb0[72:96, 0, :]).then_inc(tail_st, 16)
            for b in range(1, NB):
                i, o = (b + 3) // 4, (b + 3) % 4 * CT_TILES
                sp.dma_start(csv[b], tb0[o:o + CT_TILES, i, :]).then_inc(tail_st, 16)
            sp.wait_ge(tail_c, 2)
            sp.dma_start(outs["new_sconv_p"][0, 0].rearrange("r (t c) -> (r t) c", c=P), tb1[0:32, 0, :]).then_inc(tail_st, 16)
            ssv = outs["new_sconv_s"][0, :, PRE1 - 1, :].rearrange("b (t c) -> b t c", c=P)
            for b in range(NB):
                i, o = (b + 2) // 5, (b + 2) % 5 * TILES
                sp.dma_start(ssv[b], tb1[o:o + TILES, i, :]).then_inc(tail_st, 16)

            for t in range(5):
                sp.wait_ge(fin_ev, t + 1)
                sp.wait_ge(evac_a, t + 1)
                if t < 4:
                    sp.dma_start(outs["y_prompt"][0, t * P:(t + 1) * P, :], x_nat[t]).then_inc(y_st, 16)
                else:
                    sp.dma_start(outs["y_sample"][:, 0, :], x_nat[4]).then_inc(y_st, 16)
            sp.wait_ge(y_st, 5 * 16)
            sp.wait_ge(tail_st, 18 * 16)
            sp.wait_ge(direct_st, 2 * 16)

        @block.gpsimd
        def _(pool):
            pool.memset(ident[:, :], 0.0).then_inc(consts, 1)
            pool.memset(mask[:, :], 1.0).then_inc(consts, 1)
            pool.wait_ge(consts, 2)
            pool.affine_select(out=ident[:, :], in_=ident[:, :], compare_op=ALU.not_equal, fill=1.0, base=0,
                               pattern=[[-1, P]], channel_multiplier=1).then_inc(consts, 1)
            pool.affine_select(out=mask[:, :], in_=mask[:, :], compare_op=ALU.is_ge, fill=0.0, base=0,
                               pattern=[[1, Q]], channel_multiplier=-1).then_inc(consts, 1)
            pool.memset(ones[:, :], 1.0).then_inc(consts, 1)
            pool.memset(eps[:, :], EPS).then_inc(consts, 1)
            pool.memset(ext[:, :, 0:PRE0], 0.0).then_inc(consts, 1)
            pool.dma_start(rowsA[0:96, :], ins["ssd_conv_w"][0].rearrange("k (t c) -> (k t) c", c=P)).then_inc(par_in, 16)
            pool.dma_start(rowsA[96:120, :], ins["ssd_conv_b"][0].rearrange("(t c) -> t c", c=P)).then_inc(par_in, 16)
            pool.dma_start(rowsA[120:128, :], ins["norm_w"][0].rearrange("(t c) -> t c", c=P)).then_inc(par_in, 16)
            pool.dma_start(rowsB[0:8, :], ins["norm_w"][1].rearrange("(t c) -> t c", c=P)).then_inc(par_in, 16)
            pool.dma_start(rowsB[8:16, :], ins["final_norm_w"].rearrange("(t c) -> t c", c=P)).then_inc(par_in, 16)
            pool.dma_start(rowsB[16:32, :], ins["ssd_norm_w"][0].rearrange("(t c) -> t c", c=P)).then_inc(par_in, 16)
            pool.dma_start(rowsB[32:80, :], ins["sc_conv_w"][0].rearrange("k (t c) -> (k t) c", c=P)).then_inc(par_in, 16)
            pool.dma_start(hcol[:, 0:1], ins["ssd_dt_bias"].rearrange("a h -> h a")).then_inc(par_in, 16)
            pool.dma_start(hcol[:, 1:2], ins["ssd_A_log"].rearrange("a h -> h a")).then_inc(par_in, 16)
            pool.dma_start(dbc[:, :], ins["ssd_D"][0].partition_broadcast(P)).then_inc(par_in, 16)
            pool.dma_start(cs_nat, ins["state_ssm_conv"][0].rearrange("b k c -> (b k) c")).then_inc(cs_in, 16)
            pool.dma_start(ss_nat, ins["state_sconv"][0].rearrange("b k c -> (b k) c")).then_inc(cs_in, 16)
            pool.memset(sqs[:, :, :], 0.0).then_inc(sqs_zero, 1)
            pool.sem_inc(lo_done, SLOT)
            pool.sem_inc(sqs_done, 1)

            def low(n, slot, turn):
                pool.wait_ge(hi_done, n + (1 + SLOT))
                pool.wait_ge(raw_in[slot % RAW], turn)
                pool.tensor_tensor(wlo[:, slot, :], raw[:, slot % RAW, :], whi[:, slot, :].bitcast(F32), ALU.subtract).then_inc(lo_done, 1)

            def odd_low(k):
                pool.wait_ge(h_hi, k + 1)
                pool.tensor_tensor(hlo[:, k, :], htmp[k % 4], hhi[:, k, :].bitcast(F32), ALU.subtract).then_inc(h_lo_p, 1)

            pool.wait_ge(dtw_hi, 1)
            pool.tensor_tensor(dwl[:, :, :], dwr[:, :, :], dwh[:, :, :].bitcast(F32), ALU.subtract).then_inc(dtw_lo, 1)
            low(0, 0, 16)
            low(1, 1, 16)
            for k in range(1, KT, 2):
                odd_low(k)
            for n in range(2, SLOT):
                if n == SLOT - 1:
                    pool.wait_ge(dt_mm, 1)
                low(n, n, (n // RAW + 1) * 16)

            pool.wait_ge(sqs_zero, 1)
            with pool.Fori(0, GROUPS // 2) as G:
                for gg in range(2):
                    g = group_half(G, gg)

                    def next_low(m):
                        i = gg * 10 + m
                        pool.wait_ge(proj_done, G * 20 + (i + 1))
                        low(G * 20 + (i + SLOT), i % SLOT, G * 160 + ((i + SLOT) // RAW + 1) * 16)

                    def weigh(q):
                        pool.wait_ge(xd_done, g * 4 + (q + 1))
                        scale = dte[:, :, ds(g * 8 + 2 * q, 2)].unsqueeze(3).broadcast_to([P, NC, 2, HD])
                        pool.sem_inc(turnstile_p, 1)
                        pool.tensor_tensor(xdd[:, :, :].rearrange("p c (h d) -> p c h d", h=2),
                                           xd[:, :, :].rearrange("p c (h d) -> p c h d", h=2), scale, ALU.mult).then_inc(xdd_done, 1)

                    def inject(q):
                        pool.wait_ge(dtx_done, g * 4 + (q + 1))
                        pool.wait_ge(yr_done, g * 4 + (q + 1))
                        if q == 0:
                            pool.wait_ge(bcbc_in, g * 16 + 16)
                        pool.tensor_tensor(tdec[:, :, :], bcbc[:, :, 0, :], dtx[:, q % 2, :].unsqueeze(2).broadcast_to([P, NB, NS]),
                                           ALU.mult).then_inc(t1_done, 1)

                    def read_out(q):
                        pool.wait_ge(st_new, g * 4 + (q + 1))
                        pool.tensor_tensor(tdec[:, :, :], st[:, q % 2, :].rearrange("p (b n) -> p b n", n=NS),
                                           bcbc[:, :, 1, :], ALU.mult).then_inc(t2_done, 1)

                    def add_squares(q):
                        if q < 3:
                            pool.wait_ge(sq_done, g * 3 + (q + 1))
                        else:
                            pool.wait_ge(gate_done, g * 4 + (q + 3))
                            pool.wait_ge(sqs_done, g * 4 + (q + 1))
                            yt = ybuf[:, ds(g * 4 + q, 1), :].squeeze(1)
                            pool.sem_inc(turnstile_p, 1)
                            pool.tensor_tensor(sqb[:, :], yt, yt, ALU.mult).then_inc(sqp_done, 1)
                            pool.wait_ge(sqp_done, g + 1)
                        if q > 0:
                            pool.wait_ge(sqs_done, g * 4 + (q + 1))
                        ss = sqs[:, ds(g, 1), :].squeeze(1)
                        pool.sem_inc(turnstile_p, 1)
                        pool.tensor_tensor(ss, ss, sqb[:, :], ALU.add).then_inc(sqs_done, 1)

                    next_low(0)
                    next_low(1)
                    next_low(2)
                    weigh(0)
                    next_low(3)
                    next_low(4)
                    weigh(1)
                    next_low(5)
                    inject(0)
                    read_out(0)
                    weigh(2)
                    inject(1)
                    next_low(6)
                    read_out(1)
                    next_low(7)
                    weigh(3)
                    add_squares(0)
                    inject(2)
                    read_out(2)
                    next_low(8)
                    inject(3)
                    add_squares(1)
                    read_out(3)
                    next_low(9)
                    add_squares(2)
                    add_squares(3)

            with pool.Fori(0, 2) as half:
                for c in range(8):
                    pool.wait_ge(proj_done, half * 8 + (OUT0 + c + 1))
                    low(half * 8 + (OUT0 + c + SLOT), c % SLOT, half * 64 + ((OUT0 + c + SLOT) // RAW + 1) * 16)
            with pool.Fori(0, TILES) as j:
                for m in range(4):
                    pool.wait_ge(proj_done, j * 4 + (IN1 + m + 1))
                    low(j * 4 + (IN1 + m + SLOT), m, j * 32 + ((IN1 + m + SLOT) // RAW + 1) * 16)
            for n in range(OUT1, CHUNKS - SLOT):
                pool.wait_ge(proj_done, n + 1)
                low(n + SLOT, n % SLOT, ((n + SLOT) // RAW + 1) * 16)

        @block.scalar
        def _(act):
            act.sem_inc(hi_done, SLOT)
            act.sem_inc(proj_free, 2)
            act.sem_inc(fin_st, 16)
            for s in range(2):
                act.sem_inc(st_st[s], 16)
            act.sem_inc(ech_done, 1)
            act.sem_inc(bcd_out, 16)

            act.dma_start(x_nat[4], x_sample[:, 0, :]).then_inc(x_in[4], 16)
            def logs(parts, n):
                for dst, src in parts:
                    ln = act.activation(dst, src, ACT.Ln, scale=1.0 / n, bias=eps[0:dst.shape[0], 0:1])
                ln.then_inc(ln_done, 1)

            def roots(parts, done, count):
                act.wait_ge(ln_done, count)
                for dst, _ in parts:
                    ex = act.activation(dst, dst, ACT.Exp, scale=-0.5)
                ex.then_inc(done, 1)

            def group_parts(g):
                a, b = stat_banks[g]
                return (sqs[:, g, 0:TH], a[:, 0:TH]), (sqs[:, g, TH:T], b[:, 0:TH])

            def high(n, slot, turn):
                act.wait_ge(raw_in[slot % RAW], turn)
                act.activation(whi[:, slot, :], raw[:, slot % RAW, :], ACT.Copy).then_inc(hi_done, 1)

            for t in range(5):
                rows = P if t < 4 else NB
                act.wait_ge(x_in[t], 16)
                if t > 0:
                    act.wait_ge(ssq_done, t)
                act.activation(sqj[0:rows, :], x_nat[t], ACT.Square, accum_out=ssq[0:rows, t:t + 1]).then_inc(ssq_done, 1)
            act.wait_ge(consts, 7)
            act.wait_ge(ssq_done, 5)
            parts = (ssq[:, 0:4],) * 2, (ssq[0:NB, 4:5],) * 2
            logs(parts, D)
            roots(parts, rms_done, 1)
            act.wait_ge(dtw_in, 16)
            act.activation(dwh[:, :, :], dwr[:, :, :], ACT.Copy).then_inc(dtw_hi, 1)
            high(0, 0, 16)
            high(1, 1, 16)
            for k in range(KT):
                act.wait_ge(h_full, k + 1)
                act.activation(hhi[:, k, :], htmp[k % 4], ACT.Copy).then_inc(h_hi, 1)
            act.wait_ge(cs_t, 3)
            for i in range(2):
                act.activation(cst0[:, i * 12:(i + 1) * 12, :, :].rearrange("p t b k -> p (t b k)"),
                               bank[i][:, 0:288], ACT.Copy).then_inc(cs_c, 1)
            act.activation(cst1[:, :, :, :].rearrange("p t b k -> p (t b k)"), bank[2][:, 0:256], ACT.Copy).then_inc(cs_c, 1)
            high(2, 2, 32)

            act.wait_ge(par_in, 160)
            act.activation(hcol[:, 2:3], hcol[:, 1:2], ACT.Exp).then_inc(dt_s, 1)
            act.wait_ge(dt_v, 2)
            act.activation(dta, dtv, ACT.Abs).then_inc(dt_s, 1)
            act.wait_ge(dt_s, 2)
            act.activation(dte_, dta, ACT.Exp, scale=-1.0).then_inc(dt_s, 1)
            act.wait_ge(dt_v, 4)
            act.activation(dtl, dtw, ACT.Ln).then_inc(dt_s, 1)
            act.wait_ge(dt_s, 4)
            act.activation(dtT, dtl, ACT.Exp, scale=-1.0).then_inc(dt_s, 1)
            act.wait_ge(dt_mm, 1)
            high(SLOT - 1, SLOT - 1, ((SLOT - 1) // RAW + 1) * 16)
            act.wait_ge(dt_v, 10)
            act.activation(sm[:, 4 + NB:4 + 2 * NB], dta[:, SEQ:T], ACT.Exp).then_inc(dt_s, 1)
            act.wait_ge(dt_v, 16)
            act.dma_start(a_dram, aT).then_inc(a_out, 16)
            act.wait_ge(col_t, 1)
            act.activation(acol[:, :, :].rearrange("p c h -> p (c h)"), bank[7][:, 0:P], ACT.Copy).then_inc(dt_s, 1)
            act.activation(dtcol[:, :, :].rearrange("p c h -> p (c h)"), bank[7][:, P:2 * P], ACT.Copy).then_inc(dt_s, 1)
            act.wait_ge(dt_v, 17)
            act.activation(cdbc[:, :, :].rearrange("p c h -> p (c h)"), bank[4][:, 0:NC * HEADS], ACT.Exp).then_inc(dt_s, 1)
            act.activation(dte[:, :, :], dte[:, :, :], ACT.Exp).then_inc(dt_s, 1)
            act.wait_ge(a_out, 16)
            act.wait_ge(dt_s, 10)
            act.wait_ge(cs_c, 3)

            with act.Fori(0, GROUPS // 2) as G:
                for gg in range(2):
                    g = group_half(G, gg)

                    def split_next(m):
                        i = gg * 10 + m
                        high(G * 20 + (i + SLOT), i % SLOT, G * 160 + ((i + SLOT) // RAW + 1) * 16)

                    def evac_conv(m, tile):
                        i = gg * 10 + m
                        e = CONVED.index(ORDER[m])
                        b0, b1 = bank[2 * (m % 2)], bank[2 * (m % 2) + 1]
                        row = ext[:, e % 2, :]
                        act.wait_ge(proj_done, G * 20 + (i + 1))
                        act.activation(row[:, PRE0:PRE0 + TH], b0[:, 0:TH], ACT.Copy)
                        act.activation(row[:, PRE0 + TH:PRE0 + SEQ], b1[:, 0:SEQ - TH], ACT.Copy)
                        act.activation(dec4(row)[:, :, PRE0], b1[:, SEQ - TH:TH], ACT.Copy)
                        act.activation(tail0[:, :, ds(tile, 1)].squeeze(2), b1[:, SEQ - TH - PRE0:TH], ACT.Copy)
                        act.activation(dec4(row)[:, :, 0:PRE0], cst0[:, ds(tile, 1), :, :].squeeze(1), ACT.Copy).then_inc(proj_free, 1)
                        act.wait_ge(proj_free, G * 20 + (i + 3))
                        act.wait_ge(silu_done, g * 6 + (e + 1))
                        act.activation(acc[:, :], row[:, 0:CONV0], ACT.Identity, scale=cw0(0, tile), bias=cb0(tile)).then_inc(tap0_done, 1)
                        split_next(m)

                    def tanh_conv(e):
                        act.wait_ge(conv_done, g * 6 + (e + 1))
                        act.wait_ge(silu_done, g * 6 + (e + 1))
                        act.activation(thx[:, :], acc[:, :], ACT.Tanh).then_inc(tanh_done, 1)

                    def evac_z(m, q):
                        i = gg * 10 + m
                        b0, b1 = bank[2 * (m % 2)], bank[2 * (m % 2) + 1]
                        act.wait_ge(proj_done, G * 20 + (i + 1))
                        act.wait_ge(gate_done, g * 4 + (q + 1))
                        act.activation(zh[:, q % 2, 0:TH], b0[:, 0:TH], ACT.Copy, scale=0.5)
                        act.activation(zh[:, q % 2, TH:T], b1[:, 0:TH], ACT.Copy, scale=0.5).then_inc(proj_free, 1)
                        split_next(m)
                        act.wait_ge(proj_free, G * 20 + (i + 3))
                        act.wait_ge(sz_done, g * 4 + (q + 1))
                        act.activation(th[:, :], zh[:, q % 2, :], ACT.Tanh).then_inc(zt_done, 1)

                    def load_abc(q):
                        act.wait_ge(ech_done, g * 4 + (q + 1))
                        act.dma_start(abc[:, :, :], a_dram[ds(g * 8 + 2 * q, 2), :].partition_broadcast(P)).then_inc(abc_in, 16)

                    def segments(q):
                        act.wait_ge(abc_in, g * 64 + 16 * (q + 1))
                        act.wait_ge(sd_done, g * 4 + (q + 1))
                        for h in range(2):
                            for c in range(NC):
                                e = act.activation(em[:, h, c * Q:(c + 1) * Q], abc[:, h, c * Q:(c + 1) * Q], ACT.Relu,
                                                   scale=-1.0, bias=acol[:, c, ds(g * 8 + (2 * q + h), 1)])
                        e.then_inc(seg_done, 1)

                    def decay(q):
                        act.wait_ge(seg_done, g * 4 + (q + 1))
                        act.activation(em[:, :, :], em[:, :, :], ACT.Exp, scale=-1.0).then_inc(e_done, 1)

                    def decay_channels(q):
                        act.wait_ge(yo_done, g * 4 + (q + 1))
                        act.activation(ech[0:HD, Q:SEQ], abc[0:HD, 0, Q:SEQ], ACT.Exp)
                        act.activation(ech[HD:P, Q:SEQ], abc[HD:P, 1, Q:SEQ], ACT.Exp).then_inc(ech_done, 1)

                    def final_state(q):
                        act.wait_ge(fin_done, g * 4 + (q + 2))
                        act.dma_start(fin_out[ds(g * 512 + q * P, P), :], finb[:, :]).then_inc(fin_st, 16)

                    def load_state(q):
                        act.wait_ge(st_st[q % 2], g * 32 + 16 * (q // 2 + 1))
                        if q >= 2:
                            act.wait_ge(t2_done, g * 4 + (q - 1))
                        act.dma_start(st[:, q % 2, :].rearrange("p (b n) -> p b n", n=NS),
                                      st_in[ds(g * 512 + q * P, P), :, :]).then_inc(st_ld[q % 2], 16)

                    def scale_state(q):
                        act.wait_ge(st_ld[q % 2], g * 32 + 16 * (q // 2 + 1))
                        for b in range(NB):
                            s = st[:, q % 2, b * NS:(b + 1) * NS]
                            d = act.activation(s, s, ACT.Copy, scale=dcf[:, ds(g * (4 * NB) + (q * NB + b), 1)])
                        d.then_inc(dh_done, 1)

                    def store_state(q):
                        act.wait_ge(st_new, g * 4 + (q + 1))
                        act.dma_start(st_out[ds(g * 512 + q * P, P), :, :],
                                      st[:, q % 2, :].rearrange("p (b n) -> p b n", n=NS)).then_inc(st_st[q % 2], 16)

                    def squares(q):
                        act.wait_ge(gate_done, g * 4 + (q + 3))
                        act.wait_ge(sqs_done, g * 4 + (q + 1))
                        act.activation(sqb[:, :], ybuf[:, ds(g * 4 + q, 1), :].squeeze(1), ACT.Square).then_inc(sq_done, 1)

                    load_abc(0)
                    evac_conv(0, g + TILES)
                    tanh_conv(0)
                    evac_conv(1, g + (TILES + GROUPS))
                    tanh_conv(1)
                    evac_conv(2, g * 4)
                    segments(0)
                    tanh_conv(2)
                    act.wait_ge(tb_done, g + 1)
                    act.activation(Bs[:, :, :].rearrange("p c n -> p (c n)"), bank[4][:, :], ACT.Copy).then_inc(bs_done, 1)
                    decay(0)
                    evac_conv(3, g * 4 + 1)
                    decay_channels(0)
                    load_abc(1)
                    act.wait_ge(bcd_done, g + 1)
                    act.dma_start(bc_dram[ds(g, 1), :, :].squeeze(0), bcd[:, :, :].rearrange("b a n -> b (a n)")).then_inc(bcd_out, 16)
                    tanh_conv(3)
                    load_state(0)
                    load_state(1)
                    evac_conv(4, g * 4 + 2)
                    segments(1)
                    act.wait_ge(bcd_out, g * 16 + 32)
                    act.dma_start(bcbc[:, :, :, :].rearrange("p b a n -> p b (a n)"),
                                  bc_dram[ds(g, 1), :, :].squeeze(0).partition_broadcast(P)).then_inc(bcbc_in, 16)
                    decay(1)
                    tanh_conv(4)
                    evac_conv(5, g * 4 + 3)
                    decay_channels(1)
                    final_state(0)
                    load_abc(2)
                    scale_state(0)
                    segments(2)
                    store_state(0)
                    tanh_conv(5)
                    decay(2)
                    scale_state(1)
                    evac_z(6, 0)
                    final_state(1)
                    decay_channels(2)
                    load_abc(3)
                    load_state(2)
                    store_state(1)
                    evac_z(7, 1)
                    segments(3)
                    decay(3)
                    squares(0)
                    scale_state(2)
                    decay_channels(3)
                    load_state(3)
                    squares(1)
                    final_state(2)
                    evac_z(8, 2)
                    scale_state(3)
                    final_state(3)
                    store_state(2)
                    evac_z(9, 3)
                    store_state(3)
                    squares(2)

            act.wait_ge(tail_t, 1)
            act.activation(tb0[:, 0:2, :], bank[7][0:96, 0:2 * P].rearrange("p (i c) -> p i c", c=P), ACT.Copy)
            act.activation(tb0[0:72, 2, :], bank[7][0:72, 2 * P:3 * P], ACT.Copy).then_inc(tail_c, 1)
            for g in range(3):
                act.wait_ge(stat_mm, g + 1)
                logs(group_parts(g), DI // GROUPS)
            for g in range(3):
                roots(group_parts(g), rs_done, g + 2)

            def out_phase(base, layer):
                def x_square(k):
                    act.wait_ge(out_evac, 8 * layer + 4 + k + 1)
                    if k > 1:
                        act.wait_ge(xsum_done, 7 * layer + k - 1)
                    act.activation(sqs[:, 0, :] if k == 0 else sqb[:, :], xT[:, k, :], ACT.Square).then_inc(sq_done, 1)

                def x_weigh(k):
                    if layer == 0:
                        act.wait_ge(proj_done, base + 13 + k // 2)
                        act.activation(hhi[:, k, :], xT[:, k, :], ACT.Copy, scale=colB[:, n1 + k:n1 + k + 1]).then_inc(h_hi, 1)
                    else:
                        act.wait_ge(sq_done, 3 * GROUPS + KT + k + 1)
                        act.activation(xT[:, k, :], xT[:, k, :], ACT.Copy, scale=colB[:, nf + k:nf + k + 1]).then_inc(wf_done, 1)

                def y_high(r):
                    if layer == 0 and r < TILES:
                        act.wait_ge(ys_done, r + 1)
                    if layer == 1 and r < TILES:
                        act.wait_ge(bg_free, r + 2)
                    act.wait_ge(proj_done, base if r < 8 else base + (r - 8) // 2 + 1)
                    act.activation(hhi[:, r % 8, :], ybuf[:, r % TILES, :], ACT.Copy).then_inc(y_hi, 1)
                for r in range(8):
                    y_high(r)
                    if layer == 0 and r == 1:
                        act.wait_ge(stat_mm, 4)
                        logs(group_parts(3), DI // GROUPS)
                        roots(group_parts(3), rs_done, 5)
                    if layer == 1 and r == 1:
                        act.wait_ge(tail_t, 2)
                        act.activation(tb1[:, :, :], bank[5][0:80, 0:2 * P].rearrange("p (i c) -> p i c", c=P), ACT.Copy).then_inc(tail_c, 1)
                def next_high(c):
                    n = base + c + SLOT
                    if n < CHUNKS:
                        act.wait_ge(proj_done, base + c + 1)
                        high(n, n % SLOT, (n // RAW + 1) * 16)
                for c in range(15):
                    next_high(c)
                    if 2 * c + 8 < 32:
                        y_high(2 * c + 8)
                        y_high(2 * c + 9)
                    if 9 <= c < 13:
                        x_square(c - 9)
                    if 12 <= c < 14:
                        x_weigh(2 * c - 24)
                        x_weigh(2 * c - 23)
                for k in range(4, KT):
                    if layer == 0:
                        act.wait_ge(out_evac, 4 + k + 1)
                        x_weigh(k)
                    else:
                        x_square(k)
                        x_weigh(k)
                next_high(15)
                if layer == 0:
                    for k in range(4, KT):
                        x_square(k)

            out_phase(OUT0, 0)

            act.wait_ge(stat_mm, GROUPS + 1)
            parts = (sqs[:, 1, 0:TH], bank[6][:, 0:TH]), (sqs[:, 1, TH:T], bank[7][:, 0:TH])
            logs(parts, D)
            roots(parts, rs_done, GROUPS + 2)

            with act.Fori(0, TILES) as j:
                for m in range(4):
                    act.wait_ge(proj_done, j * 4 + (IN1 + m + 1))
                    high(j * 4 + (IN1 + m + SLOT), m, j * 32 + ((IN1 + m + SLOT) // RAW + 1) * 16)
                    if m == 0:
                        act.wait_ge(z_free, j + 2)
                        act.wait_ge(slr_done, j + 1)
                        act.activation(th[:, :], zh[:, 1, :], ACT.Silu).then_inc(sl_done, 1)

            out_phase(OUT1, 1)

            act.wait_ge(col_sq, 1)
            parts = (ssq[:, 0:4], bank[7][:, 0:4]), (ssq[0:NB, 4:5], bank[7][0:NB, 4:5])
            logs(parts, D)
            roots(parts, col_rms, GROUPS + 3)
            act.wait_ge(col_rms, 1)
            for t in range(5):
                rows = P if t < 4 else NB
                act.wait_ge(fin_tr, t + 1)
                act.activation(x_nat[t][:, 0:512], bank[2 * t % 8][0:rows, :], ACT.Copy, scale=ssq[0:rows, t:t + 1]).then_inc(fin_ev, 1)
            act.wait_ge(fin_st, 16 * 17)
            for s in range(2):
                act.wait_ge(st_st[s], 16 * 9)

        @block.vector
        def _(dve):
            dve.sem_inc(silu_done, 1)
            dve.sem_inc(yo_done, 1)
            dve.sem_inc(gate_done, 2)
            dve.sem_inc(yr_done, 1)
            dve.sem_inc(fin_done, 1)
            dve.sem_inc(yd_done, 1)
            dve.sem_inc(sz_done, 1)
            dve.sem_inc(out_evac, 4)
            for s in (cg_free, xin_free, z_free, bg_free, slr_done):
                dve.sem_inc(s, 1)

            for k in range(KT):
                dve.wait_ge(xt_done, k + 1)
                dve.tensor_copy(xT[:, k, 0:SEQ], bank[k][:, :]).then_inc(xt_out, 1)
            dve.wait_ge(xt_done, KT + 1)
            dve.tensor_copy(xT[:, :, SEQ:T], bank[4][:, 0:KT * NB].rearrange("p (k b) -> p k b", b=NB)).then_inc(xt_out, 1)
            dve.wait_ge(rms_done, 1)
            dve.wait_ge(consts, 7)
            for t in range(4):
                dve.tensor_scalar(xdd[:, t, :], ident[:, :], ssq[:, t:t + 1], None, ALU.mult).then_inc(diag_done, 1)
            dve.tensor_scalar(finb[0:NB, 0:NB], ident[0:NB, 0:NB], ssq[0:NB, 4:5], None, ALU.mult).then_inc(diag_done, 1)
            dve.wait_ge(par_t, 1)
            dve.tensor_scalar(colA[:, 0:n0], bank[7][:, 0:n0], 0.5, None, ALU.mult)
            dve.tensor_copy(colA[:, n0:P], bank[7][:, n0:P])
            dve.tensor_copy(colB[:, :], bank[7][:, P:P + 80]).then_inc(par_c, 1)
            dve.wait_ge(par_c, 1)
            dve.wait_ge(rb_done, 1)
            dve.tensor_copy(rb0[:, 0:SEQ], bank[5][:, :])
            dve.tensor_copy(rb0[:, SEQ:T], bank[6][:, 0:NB]).then_inc(rb_out, 1)
            dve.wait_ge(rb_out, 1)
            dve.wait_ge(xt_out, KT + 1)
            def full(k):
                if k >= 4:
                    dve.wait_ge(h_hi, k - 3)
                    if k % 2:
                        dve.wait_ge(h_lo_p, (k - 4) // 2 + 1)
                    else:
                        dve.wait_ge(h_lo, (k - 4) // 2 + 1)
                dve.scalar_tensor_tensor(htmp[k % 4], xT[:, k, :], colA[:, n0 + k:n0 + k + 1], rb0[:, :],
                                         ALU.mult, ALU.mult).then_inc(h_full, 1)

            for k in range(0, KT, 2):
                full(k)
                full(k + 1)
                dve.wait_ge(h_hi, k + 1)
                dve.wait_ge(h_full, k + 1)
                dve.tensor_tensor(hlo[:, k, :], htmp[k % 4], hhi[:, k, :].bitcast(F32), ALU.subtract).then_inc(h_lo, 1)

            dve.wait_ge(par_in, 160)
            dve.wait_ge(dt_mm, 1)
            dve.tensor_scalar(dtv[:, 0:TH], bank[6][0:HEADS, 0:TH], hcol[:, 0:1], None, ALU.add).then_inc(dt_v, 1)
            dve.tensor_scalar(dtv[:, TH:T], bank[7][0:HEADS, 0:TH], hcol[:, 0:1], None, ALU.add).then_inc(dt_v, 1)
            dve.wait_ge(dt_s, 1)
            dve.tensor_scalar(hcol[:, 3:4], hcol[:, 2:3], -1.0, None, ALU.mult).then_inc(dt_v, 1)
            dve.wait_ge(dt_s, 3)
            dve.tensor_scalar(dtw, dte_, 1.0, None, ALU.add).then_inc(dt_v, 1)
            dve.wait_ge(dt_v, 4)
            dve.tensor_scalar(dta, dtw, -1.0, None, ALU.add).then_inc(dt_v, 1)
            dve.wait_ge(dt_v, 5)
            dve.tensor_tensor(dte_, dte_, dta, ALU.subtract).then_inc(dt_v, 1)
            dve.wait_ge(dt_s, 5)
            dve.wait_ge(dt_v, 6)
            dve.tensor_tensor(dte_, dte_, dtT, ALU.mult).then_inc(dt_v, 1)
            dve.scalar_tensor_tensor(dtl, dtv, 0.0, dtl, ALU.max, ALU.add).then_inc(dt_v, 1)
            dve.wait_ge(dt_v, 8)
            dve.tensor_tensor(dtT, dtl, dte_, ALU.add).then_inc(dt_v, 1)
            dve.wait_ge(dt_v, 9)
            dve.tensor_scalar(dta, dtT, hcol[:, 3:4], None, ALU.mult).then_inc(dt_v, 1)
            dve.wait_ge(dt_v, 10)
            for c in range(NC):
                dve.tensor_tensor_scan(aT[:, c * Q:(c + 1) * Q], ones[0:HEADS, :], dta[:, c * Q:(c + 1) * Q], 0.0,
                                       ALU.mult, ALU.add).then_inc(dt_v, 1)
            dve.wait_ge(dt_v, 14)
            dve.tensor_copy(sm[:, 0:4], aT.rearrange("p (c l) -> p c l", l=Q)[:, :, Q - 1]).then_inc(dt_v, 1)
            dve.tensor_copy(sm[:, 4:4 + NB], dtT[:, SEQ:T]).then_inc(dt_v, 1)
            dve.wait_ge(dt_v, 16)
            dve.wait_ge(dt_s, 6)
            dve.tensor_tensor(smd[:, :, :], ident[0:HEADS, 0:HEADS].unsqueeze(1).broadcast_to([HEADS, SMN, HEADS]),
                              sm[:, :].unsqueeze(2).broadcast_to([HEADS, SMN, HEADS]), ALU.mult).then_inc(smd_done, 1)
            dve.wait_ge(smb_done, 1)
            dve.wait_ge(dt_s, 7)
            dve.tensor_tensor(dte[:, :, :], bank[4][:, 0:NC * HEADS].rearrange("p (c h) -> p c h", h=HEADS), acol[:, :, :],
                              ALU.subtract).then_inc(dt_v, 1)
            for half, lo in ((0, 0), (1, HD)):
                rows = slice(lo, lo + HD)
                by = bank[5][rows, 0:2 * NB * HEADS].rearrange("p (v j h) -> p h j v", h=2, j=TILES)[:, half, :, :]
                dve.tensor_copy(dtch[rows, :, :], by[:, :, 0:NB]).then_inc(dt_v, 1)
                dve.tensor_copy(dcch[rows, :, :], by[:, :, NB:2 * NB]).then_inc(dt_v, 1)
                dve.tensor_copy(dch[rows, :], dbc[rows, :].rearrange("p (j h) -> p j h", h=2)[:, :, half]).then_inc(dt_v, 1)
            dve.wait_ge(dt_v, 23)
            dve.wait_ge(dt_s, 10)

            with dve.Fori(0, GROUPS // 2) as G:
                for gg in range(2):
                    g = group_half(G, gg)

                    def conv(m, tile):
                        i = gg * 10 + m
                        e = CONVED.index(ORDER[m])
                        row = ext[:, e % 2, :]
                        dve.wait_ge(tap0_done, g * 6 + (e + 1))
                        for k in range(1, TAPS0):
                            if k > 1:
                                dve.wait_ge(tap, g * 12 + (2 * e + k - 1))
                            t = dve.scalar_tensor_tensor(acc[:, :], row[:, k:k + CONV0], cw0(k, tile), acc[:, :], ALU.mult, ALU.add)
                            t.then_inc(tap if k < 3 else conv_done, 1)

                    def silu(e, dst):
                        dve.wait_ge(tanh_done, g * 6 + (e + 1))
                        dve.wait_ge(conv_done, g * 6 + (e + 1))
                        if e >= 4:
                            dve.wait_ge(yd_done, g * 8 + (2 * e - 5))
                            dve.wait_ge(dtx_done, g * 4 + (e - 3))
                        dve.scalar_tensor_tensor(dst, thx[:, :], 1.0, acc[:, :], ALU.add, ALU.mult).then_inc(silu_done, 1)

                    def weigh_dt(q):
                        dve.wait_ge(t_done, g * 4 + (q + 1))
                        scale = dtcol[:, :, ds(g * 8 + 2 * q, 2)].unsqueeze(3).broadcast_to([P, NC, 2, HD])
                        dve.tensor_tensor(xd[:, :, :].rearrange("p c (h d) -> p c h d", h=2),
                                          bank[4][:, :].rearrange("p (c h d) -> p c h d", c=NC, h=2), scale, ALU.mult).then_inc(xd_done, 1)

                    def causal(q):
                        dve.wait_ge(e_done, g * 4 + (q + 1))
                        if q == 0:
                            dve.wait_ge(cbm_done, g + 1)
                        cbm = CBm[:, :, :].rearrange("p c l -> p (c l)").unsqueeze(1).broadcast_to([P, 2, SEQ])
                        dve.tensor_tensor(em[:, :, :], em[:, :, :], cbm, ALU.mult).then_inc(m_done, 1)

                    def recur(q):
                        dve.wait_ge(s_done, g * 4 + (q + 1))
                        dve.tensor_copy(hs[:, 0, :], bank[5][:, 0:P]).then_inc(rec, 1)
                        for c in range(1, NC):
                            dve.wait_ge(rec, g * 28 + (7 * q + 2 * c - 1))
                            for h in range(2):
                                dve.scalar_tensor_tensor(hs[:, c, h * HD:(h + 1) * HD], hs[:, c - 1, h * HD:(h + 1) * HD],
                                                         cdbc[:, c, ds(g * 8 + (2 * q + h), 1)],
                                                         bank[5][:, c * P + h * HD:c * P + (h + 1) * HD],
                                                         ALU.mult, ALU.add).then_inc(rec, 1)

                    def skip(q):
                        dve.wait_ge(sd_done, g * 4 + (q + 2))
                        yt = ybuf[:, ds(g * 4 + q, 1), :].squeeze(1)
                        d = dch[:, ds(g * 4 + q, 1)]
                        dve.scalar_tensor_tensor(yt[:, 0:SEQ], xs[:, q % 2, 0:SEQ], d, bank[6][:, :], ALU.mult, ALU.add).then_inc(yd_done, 1)
                        dve.tensor_scalar(yt[:, SEQ:T], dec_conv(xs[:, q % 2, :]), d, None, ALU.mult).then_inc(yd_done, 1)

                    def add_earlier(q):
                        dve.wait_ge(o_done, g * 4 + (q + 1))
                        dve.wait_ge(ech_done, g * 4 + (q + 2))
                        dve.wait_ge(fin_st, g * 64 + 16 * (q + 1))
                        dve.tensor_copy(finb[:, :], bank[7][:, 0:NS]).then_inc(fin_done, 1)
                        dve.tensor_tensor(yob[:, :], bank[7][:, Q:SEQ], ech[:, Q:SEQ], ALU.mult).then_inc(yo_done, 1)
                        dve.wait_ge(yo_done, g * 4 + (q + 2))
                        dve.wait_ge(yd_done, g * 8 + (2 * q + 3))
                        yt = ybuf[:, ds(g * 4 + q, 1), :].squeeze(1)
                        dve.tensor_tensor(yt[:, Q:SEQ], yt[:, Q:SEQ], yob[:, :], ALU.add).then_inc(y_done, 1)

                    def sample_x(q):
                        dve.wait_ge(silu_done, g * 6 + (q + 4))
                        if q >= 2:
                            dve.wait_ge(t1_done, g * 4 + (q - 1))
                        dve.tensor_tensor(dtx[:, q % 2, :], dec_conv(xs[:, q % 2, :]), dtch[:, ds(g * 4 + q, 1), :].squeeze(1),
                                          ALU.mult).then_inc(dtx_done, 1)

                    def sample_add(q):
                        dve.wait_ge(t1_done, g * 4 + (q + 1))
                        dve.wait_ge(dh_done, g * 4 + (q + 1))
                        dve.tensor_tensor(st[:, q % 2, :], st[:, q % 2, :], tdf, ALU.add).then_inc(st_new, 1)

                    def sample_out(q):
                        dve.wait_ge(t2_done, g * 4 + (q + 1))
                        dve.tensor_reduce(yr[:, :], tdec[:, :, :], AX, ALU.add).then_inc(yr_done, 1)
                        dve.wait_ge(yr_done, g * 4 + (q + 2))
                        yt = ybuf[:, ds(g * 4 + q, 1), :].squeeze(1)[:, SEQ:T]
                        dve.tensor_tensor(yt, yt, yr[:, :], ALU.add).then_inc(ydec_done, 1)

                    def silu_z(q):
                        dve.wait_ge(zt_done, g * 4 + (q + 1))
                        dve.scalar_tensor_tensor(zh[:, q % 2, :], th[:, :], 1.0, zh[:, q % 2, :], ALU.add, ALU.mult).then_inc(sz_done, 1)

                    def gate(q):
                        dve.wait_ge(sz_done, g * 4 + (q + 2))
                        dve.wait_ge(y_done, g * 4 + (q + 1))
                        dve.wait_ge(ydec_done, g * 4 + (q + 1))
                        yt = ybuf[:, ds(g * 4 + q, 1), :].squeeze(1)
                        dve.tensor_tensor(yt, yt, zh[:, q % 2, :], ALU.mult).then_inc(gate_done, 1)

                    conv(0, g + TILES)
                    silu(0, BT[:, :])
                    conv(1, g + (TILES + GROUPS))
                    silu(1, CT[:, :])
                    conv(2, g * 4)
                    silu(2, xs[:, 0, :])
                    dve.wait_ge(cb_done, g + 1)
                    dve.tensor_tensor(CBm[:, :, :], bank[5][:, :].rearrange("p (c l) -> p c l", l=Q),
                                      mask[:, :].unsqueeze(1).broadcast_to([P, NC, Q]), ALU.mult).then_inc(cbm_done, 1)
                    dve.wait_ge(bct_done, g + 1)
                    dve.wait_ge(bcd_out, g * 16 + 16)
                    dve.tensor_copy(bcd[:, :, :], bank[6][0:NB, 0:2 * NS].rearrange("b (a n) -> b a n", n=NS)).then_inc(bcd_done, 1)
                    causal(0)
                    weigh_dt(0)
                    conv(3, g * 4 + 1)
                    silu(3, xs[:, 1, :])
                    recur(0)
                    skip(0)
                    weigh_dt(1)
                    sample_x(0)
                    conv(4, g * 4 + 2)
                    causal(1)
                    silu(4, xs[:, 0, :])
                    add_earlier(0)
                    recur(1)
                    conv(5, g * 4 + 3)
                    skip(1)
                    sample_add(0)
                    weigh_dt(2)
                    sample_x(1)
                    silu(5, xs[:, 1, :])
                    causal(2)
                    sample_out(0)
                    add_earlier(1)
                    sample_add(1)
                    silu_z(0)
                    recur(2)
                    skip(2)
                    sample_x(2)
                    gate(0)
                    silu_z(1)
                    weigh_dt(3)
                    sample_out(1)
                    causal(3)
                    gate(1)
                    add_earlier(2)
                    sample_add(2)
                    recur(3)
                    skip(3)
                    sample_x(3)
                    sample_out(2)
                    silu_z(2)
                    add_earlier(3)
                    sample_add(3)
                    gate(2)
                    silu_z(3)
                    sample_out(3)
                    gate(3)

            def out_phase(base, layer):
                def scale(r):
                    dve.wait_ge(rs_done, r // STEPS + 1)
                    dve.wait_ge(gate_done, TILES + 2)
                    dve.scalar_tensor_tensor(ybuf[:, r, :], ybuf[:, r, :], colB[:, ng + r:ng + r + 1], sqs[:, r // STEPS, :],
                                             ALU.mult, ALU.mult).then_inc(ys_done, 1)
                if layer == 0:
                    scale(0)
                for r in range(2 * TILES):
                    if layer == 0 and r + 1 < TILES:
                        scale(r + 1)
                    if r == TILES + 6:
                        for i in range(4):
                            residual(base, layer, 0, i)
                    dve.wait_ge(y_hi, layer * 32 + r + 1)
                    if layer == 0 and r < TILES:
                        dve.wait_ge(ys_done, r + 1)
                    if layer == 1 and r < TILES:
                        dve.wait_ge(bg_free, r + 2)
                    dve.wait_ge(proj_done, base if r < 8 else base + (r - 8) // 2 + 1)
                    dve.tensor_tensor(hlo[:, r % 8, :], ybuf[:, r % TILES, :], hhi[:, r % 8, :].bitcast(F32), ALU.subtract).then_inc(y_lo, 1)
                for k in range(1, 4):
                    add_square(layer, k)
                if layer == 0:
                    for k in range(4):
                        x_low(k)
                for i in range(4):
                    residual(base, layer, 1, i)
                    if layer == 0 and i > 0:
                        x_low(3 + i)
                    if layer == 1 and i > 0:
                        add_square(layer, 3 + i)
                if layer == 0:
                    x_low(7)
                    for k in range(4, 7):
                        add_square(layer, k)
                add_square(layer, 7)

            def residual(base, layer, half, i):
                if i < 3:
                    dve.wait_ge(out_mm, 6 * layer + 3 * half + i + 1)
                else:
                    dve.wait_ge(proj_done, base + 8 * (half + 1))
                k = 4 * half + i
                if layer == 1:
                    dve.wait_ge(h_hi, 2 * KT)
                dve.tensor_tensor(xT[:, k, 0:TH], xT[:, k, 0:TH], bank[2 * i][:, 0:TH], ALU.add)
                dve.tensor_tensor(xT[:, k, TH:T], xT[:, k, TH:T], bank[2 * i + 1][:, 0:TH], ALU.add).then_inc(out_evac, 1)

            def add_square(layer, k):
                dve.wait_ge(sq_done, 3 * GROUPS + KT * layer + k + 1)
                if k > 1:
                    dve.wait_ge(xsum_done, 7 * layer + k - 1)
                dve.tensor_tensor(sqs[:, 0, :], sqs[:, 0, :], sqb[:, :], ALU.add).then_inc(xsum_done, 1)

            def x_low(k):
                dve.wait_ge(h_hi, KT + k + 1)
                dve.wait_ge(out_evac, 4 + k + 1)
                dve.wait_ge(proj_done, OUT0 + 13 + k // 2)
                dve.scalar_tensor_tensor(hlo[:, k, :], xT[:, k, :], colB[:, n1 + k:n1 + k + 1], hhi[:, k, :].bitcast(F32),
                                         ALU.mult, ALU.subtract).then_inc(h_lo, 1)

            out_phase(OUT0, 0)

            r1, r2 = sqs[:, 1, :], sqs[:, 2, :]
            dve.wait_ge(rs_done, GROUPS + 1)
            dve.tensor_tensor(r2, r1, r1, ALU.mult).then_inc(r2_done, 1)
            dve.wait_ge(r2_done, 1)

            dve.memset(ext[:, :, 0:PRE1], 0.0).then_inc(cs1_done, 1)
            with dve.Fori(0, TILES // 2) as J:
                for jj in range(2):
                    j = J * 2 + jj
                    row = ext[:, jj, 0:EXT1]
                    dec = row[:, DEC1:EXT1].rearrange("p (b k) -> p b k", k=TAPS1)
                    u, zr, cv, c2 = zh[:, 0, :], zh[:, 1, :], acc[:, 0:CONV1], thx[:, 0:T]
                    dve.wait_ge(proj_done, j * 4 + (IN1 + 1))
                    dve.tensor_tensor(zr[:, 0:TH], bank[0][:, 0:TH], r1[:, 0:TH], ALU.mult)
                    dve.tensor_tensor(zr[:, TH:T], bank[1][:, 0:TH], r1[:, TH:T], ALU.mult).then_inc(z_free, 1)
                    dve.wait_ge(proj_done, j * 4 + (IN1 + 2))
                    dve.tensor_tensor(u[:, 0:TH], bank[2][:, 0:TH], r2[:, 0:TH], ALU.mult).then_inc(u_done, 1)
                    dve.tensor_tensor(u[:, TH:T], bank[3][:, 0:TH], r2[:, TH:T], ALU.mult).then_inc(cg_free, 1)
                    dve.tensor_copy(dec[:, :, 0:PRE1], cst1[:, ds(j, 1), :, :].squeeze(1)).then_inc(cs1_done, 1)
                    dve.wait_ge(sl_done, j + 1)
                    dve.tensor_tensor(c2, th[:, :], r1, ALU.mult).then_inc(slr_done, 1)
                    dve.wait_ge(proj_done, j * 4 + (IN1 + 3))
                    dve.wait_ge(cg_free, j + 2)
                    dve.tensor_tensor(row[:, PRE1:PRE1 + TH], bank[4][:, 0:TH], u[:, 0:TH], ALU.mult)
                    dve.tensor_tensor(row[:, PRE1 + TH:PRE1 + SEQ], bank[5][:, 0:SEQ - TH], u[:, TH:SEQ], ALU.mult)
                    dve.tensor_tensor(dec[:, :, PRE1], bank[5][:, SEQ - TH:TH], u[:, SEQ:T], ALU.mult).then_inc(xin_free, 1)
                    dve.wait_ge(xin_free, j + 2)
                    dve.tensor_scalar(cv, row[:, 0:CONV1], colB[:, ds(j + c1, 1)], None, ALU.mult).then_inc(tap1, 1)
                    dve.tensor_copy(tail1[:, 0:PRE1, ds(j, 1)].squeeze(2), row[:, SEQ:SEQ + PRE1])
                    dve.tensor_copy(tail1[:, PRE1:TAIL1, ds(j, 1)].squeeze(2), dec[:, :, PRE1]).then_inc(tail1_done, 1)
                    for k in range(1, TAPS1):
                        dve.wait_ge(tap1, j * 3 + k)
                        dve.scalar_tensor_tensor(cv, row[:, k:k + CONV1], colB[:, ds(j + (c1 + k * TILES), 1)], cv,
                                                 ALU.mult, ALU.add).then_inc(tap1, 1)
                    dve.wait_ge(tap1, j * 3 + 3)
                    dve.wait_ge(slr_done, j + 2)
                    dve.tensor_tensor(c2[:, 0:SEQ], c2[:, 0:SEQ], cv[:, 0:SEQ], ALU.mult)
                    dve.tensor_tensor(c2[:, SEQ:T], c2[:, SEQ:T], cv[:, DEC1:CONV1:TAPS1], ALU.mult).then_inc(c2_done, 1)
                    dve.wait_ge(c2_done, j + 1)
                    dve.wait_ge(proj_done, j * 4 + (IN1 + 4))
                    yt = ybuf[:, ds(j, 1), :].squeeze(1)
                    dve.tensor_tensor(yt[:, 0:TH], bank[6][:, 0:TH], c2[:, 0:TH], ALU.mult)
                    dve.tensor_tensor(yt[:, TH:T], bank[7][:, 0:TH], c2[:, TH:T], ALU.mult).then_inc(bg_free, 1)

            out_phase(OUT1, 1)

            dve.wait_ge(col_rms, 1)
            for t in range(5):
                rows = P if t < 4 else NB
                dve.wait_ge(fin_tr, t + 1)
                dve.tensor_scalar(x_nat[t][:, 512:D], bank[(2 * t + 1) % 8][0:rows, :], ssq[0:rows, t:t + 1], None,
                                  ALU.mult).then_inc(evac_a, 1)

        @block.tensor
        def _(pe):
            pe.sem_inc(sd_done, 1)

            def transpose(dst, src):
                n = src.shape[0]
                return pe.matmul(dst, src, ident[0:n, 0:n], is_transpose=True, start=True, stop=True)

            pe.wait_ge(consts, 7)
            for t in range(4):
                pe.wait_ge(x_in[t], 16)
                for k in range(KT):
                    mm = transpose(bank[k][:, t * P:(t + 1) * P], x_nat[t][:, k * P:(k + 1) * P])
                    if t == 3:
                        mm.then_inc(xt_done, 1)
            pe.wait_ge(x_in[4], 16)
            pe.wait_ge(xt_out, 5)
            for k in range(KT):
                mm = transpose(bank[4][:, k * NB:(k + 1) * NB], x_nat[4][:, k * P:(k + 1) * P])
            mm.then_inc(xt_done, 1)
            pe.wait_ge(par_in, 160)
            pe.wait_ge(xt_out, KT)
            transpose(bank[7][:, 0:P], rowsA[:, :])
            transpose(bank[7][:, P:P + 80], rowsB[:, :]).then_inc(par_t, 1)
            pe.wait_ge(diag_done, 5)
            for t in range(4):
                pe.matmul(bank[5][:, t * P:(t + 1) * P], ones[:, :], xdd[:, t, :], start=True, stop=True)
            pe.matmul(bank[6][:, 0:NB], ones[0:NB, :], finb[0:NB, 0:NB], start=True, stop=True).then_inc(rb_done, 1)
            pe.wait_ge(cs_in, 32)
            pe.wait_ge(xt_out, KT)
            for t in range(CT_TILES):
                mm = transpose(bank[t // 12][:, t % 12 * 24:(t % 12 + 1) * 24], cs_nat[:, t * P:(t + 1) * P])
                if t % 12 == 11:
                    mm.then_inc(cs_t, 1)
            for t in range(TILES):
                mm = transpose(bank[2][:, t * 16:(t + 1) * 16], ss_nat[:, t * P:(t + 1) * P])
            mm.then_inc(cs_t, 1)

            pe.wait_ge(dtw_hi, 1)
            pe.wait_ge(dtw_lo, 1)
            pe.wait_ge(rb_out, 1)
            pe.wait_ge(par_c, 1)
            for k in range(KT):
                pe.wait_ge(h_hi, k + 1)
                if k % 2:
                    pe.wait_ge(h_lo_p, k // 2 + 1)
                else:
                    pe.wait_ge(h_lo, k // 2 + 1)
                for i, (w, h) in enumerate(((dwh, hhi), (dwh, hlo), (dwl, hhi))):
                    for half in range(2):
                        mm = pe.matmul(bank[6 + half][0:HEADS, 0:TH], w[:, k, :], h[:, k, half * TH:(half + 1) * TH],
                                       start=(k == 0 and i == 0), stop=(k == KT - 1 and i == 2))
            mm.then_inc(dt_mm, 1)

            def project(n, slot, b0, b1, h_ready=None):
                pe.wait_ge(hi_done, n + (SLOT + 1))
                pe.wait_ge(lo_done, n + (SLOT + 1))
                for k in range(KT):
                    if h_ready is not None:
                        pe.wait_ge(h_hi, h_ready + k + 1)
                        pe.wait_ge(h_lo, h_ready - KT // 2 + k + 1)
                    for i, (w, h) in enumerate(((whi, hhi), (whi, hlo), (wlo, hhi))):
                        for b, cols in ((b0, slice(0, TH)), (b1, slice(TH, T))):
                            mm = pe.matmul(b[:, 0:TH], w[:, slot, k * P:(k + 1) * P], h[:, k, cols],
                                           start=(k == 0 and i == 0), stop=(k == KT - 1 and i == 2))
                mm.then_inc(proj_done, 1)

            def columns():
                pe.wait_ge(dt_v, 16)
                for c in range(NC):
                    transpose(bank[7][:, c * HEADS:(c + 1) * HEADS], aT[:, c * Q:(c + 1) * Q])
                for c in range(NC):
                    mm = transpose(bank[7][:, P + c * HEADS:P + (c + 1) * HEADS], dtT[:, c * Q:(c + 1) * Q])
                mm.then_inc(col_t, 1)
                pe.wait_ge(smd_done, 1)
                pe.matmul(bank[4][:, 0:NC * HEADS], ones[0:HEADS, :], smd[:, 0:NC, :].rearrange("p v h -> p (v h)"),
                          start=True, stop=True)
                pe.matmul(bank[5][:, 0:2 * NB * HEADS], ones[0:HEADS, :], smd[:, NC:SMN, :].rearrange("p v h -> p (v h)"),
                          start=True, stop=True).then_inc(smb_done, 1)

            def two_groups(G, first=False):
                for gg in range(2):
                    g = group_half(G, gg)

                    def proj(m):
                        i = gg * 10 + m
                        pe.wait_ge(proj_free, G * 20 + (i + 1))
                        if m == 0 and gg == 0:
                            pe.wait_ge(cs_c, 3)
                        project(G * 20 + i, i % SLOT, bank[2 * (m % 2)], bank[2 * (m % 2) + 1])

                    def group_matrices():
                        pe.wait_ge(silu_done, g * 6 + 3)
                        for c in range(NC):
                            mm = transpose(bank[4][:, c * Q:(c + 1) * Q], BT[:, c * Q:(c + 1) * Q])
                        mm.then_inc(tb_done, 1)
                        if gg == 1:
                            pe.wait_ge(rec, g * 28)
                        for c in range(NC):
                            mm = pe.matmul(bank[5][:, c * Q:(c + 1) * Q], BT[:, c * Q:(c + 1) * Q], CT[:, c * Q:(c + 1) * Q],
                                           start=True, stop=True)
                        mm.then_inc(cb_done, 1)
                        pe.wait_ge(yd_done, g * 8 + 1)
                        transpose(bank[6][0:NB, 0:NS], dec_conv(BT))
                        transpose(bank[6][0:NB, NS:2 * NS], dec_conv(CT)).then_inc(bct_done, 1)

                    def turn(q):
                        pe.wait_ge(silu_done, g * 6 + (q + 4))
                        if q == 0:
                            pe.wait_ge(bs_done, g + 1)
                        for c in range(NC):
                            mm = transpose(bank[4][:, c * Q:(c + 1) * Q], xs[:, q % 2, c * Q:(c + 1) * Q])
                        mm.then_inc(t_done, 1)

                    def within(q):
                        pe.wait_ge(xdd_done, g * 4 + (q + 1))
                        if q == 0:
                            pe.wait_ge(cbm_done, g + 1)
                        else:
                            pe.wait_ge(rec, g * 28 + 7 * q)
                        for c in range(NC):
                            mm = pe.matmul(bank[5][:, c * P:(c + 1) * P], Bs[:, c, :], xdd[:, c, :], start=True, stop=True)
                        mm.then_inc(s_done, 1)
                        pe.wait_ge(m_done, g * 4 + (q + 1))
                        if q == 0:
                            pe.wait_ge(bcd_done, g + 1)
                        else:
                            pe.wait_ge(yd_done, g * 8 + 2 * q)
                        for c in range(NC):
                            for h in range(2):
                                mm = pe.matmul(bank[6][h * HD:(h + 1) * HD, c * Q:(c + 1) * Q], xd[:, c, h * HD:(h + 1) * HD],
                                               em[:, h, c * Q:(c + 1) * Q], start=True, stop=True)
                        mm.then_inc(sd_done, 1)

                    def across(q):
                        pe.wait_ge(rec, g * 28 + 7 * (q + 1))
                        pe.wait_ge(yo_done, g * 4 + (q + 1))
                        pe.wait_ge(fin_done, g * 4 + (q + 1))
                        transpose(bank[7][:, 0:NS], hs[:, NC - 1, :])
                        for c in range(1, NC):
                            mm = pe.matmul(bank[7][:, c * Q:(c + 1) * Q], hs[:, c - 1, :], CT[:, c * Q:(c + 1) * Q],
                                           start=True, stop=True)
                        mm.then_inc(o_done, 1)

                    proj(0)
                    proj(1)
                    if first and gg == 0:
                        columns()
                    proj(2)
                    proj(3)
                    group_matrices()
                    turn(0)
                    proj(4)
                    within(0)
                    turn(1)
                    proj(5)
                    across(0)
                    within(1)
                    turn(2)
                    proj(6)
                    across(1)
                    proj(7)
                    within(2)
                    proj(8)
                    turn(3)
                    across(2)
                    within(3)
                    proj(9)
                    across(3)

            two_groups(0, first=True)
            with pe.Fori(1, GROUPS // 2) as G:
                two_groups(G)

            def group_sums(g):
                pe.wait_ge(sqs_done, STEPS * (g + 1) + 1)
                for half, b in enumerate(stat_banks[g]):
                    mm = pe.matmul(b[:, 0:TH], ones[:, :], sqs[:, g, half * TH:(half + 1) * TH], start=True, stop=True)
                mm.then_inc(stat_mm, 1)

            group_sums(0)
            pe.wait_ge(proj_free, OUT0 + 1)
            group_sums(1)
            pe.wait_ge(proj_free, OUT0 + 2)
            group_sums(2)
            pe.wait_ge(yo_done, TILES + 1)
            tf = tail0[:, :, :].rearrange("p r t -> p (r t)")
            for i in range(3):
                n = 96 if i < 2 else 72
                mm = transpose(bank[7][0:n, i * P:(i + 1) * P], tf[:, i * 96:i * 96 + n])
            mm.then_inc(tail_t, 1)
            pe.wait_ge(tail_c, 1)
            pe.wait_ge(yd_done, 2 * TILES + 1)
            group_sums(3)

            def out_phase(base, layer):
                with pe.Fori(0, 2) as half:
                    for c in range(8):
                        pe.wait_ge(hi_done, half * 8 + (base + c + SLOT + 1))
                        pe.wait_ge(lo_done, half * 8 + (base + c + SLOT + 1))
                        pe.wait_ge(y_hi, half * 16 + (32 * layer + 2 * c + 2))
                        pe.wait_ge(y_lo, half * 16 + (32 * layer + 2 * c + 2))
                        for i in range(4):
                            if c == 0:
                                pe.wait_ge(out_evac, half * 4 + (8 * layer + i + 1))
                            if c == 0 and layer == 0 and i == 3:
                                pe.wait_ge(ln_done, GROUPS + 1)
                            if c == 0 and layer == 1 and i == 2:
                                pe.wait_ge(tail_c, 2)
                            if c == 0 and layer == 1 and i == 3:
                                pe.wait_ge(bg_free, TILES + 1)
                            for kk in range(2):
                                r = (2 * c + kk) % 8
                                for v, (w, h) in enumerate(((whi, hhi), (whi, hlo), (wlo, hhi))):
                                    for hb in range(2):
                                        mm = pe.matmul(bank[2 * i + hb][:, 0:TH],
                                                       w[:, c % SLOT, kk * 512 + i * P:kk * 512 + (i + 1) * P],
                                                       h[:, r, hb * TH:(hb + 1) * TH],
                                                       start=(c == 0 and kk == 0 and v == 0),
                                                       stop=(c == 7 and kk == 1 and v == 2))
                            if c == 7 and i < 3:
                                mm.then_inc(out_mm, 1)
                        mm.then_inc(proj_done, 1)

            out_phase(OUT0, 0)

            def block1(j, first=False):
                def part(m, h_ready=None):
                    if first:
                        pe.wait_ge(out_evac, 8 + m + 1)
                    project(j * 4 + (IN1 + m), m, bank[2 * m], bank[2 * m + 1], h_ready)
                pe.wait_ge(z_free, j + 1)
                part(0, KT if first else None)
                pe.wait_ge(cg_free, j + 1)
                part(1)
                pe.wait_ge(xin_free, j + 1)
                part(2)
                if first:
                    pe.wait_ge(xsum_done, 7)
                    for half in range(2):
                        mm = pe.matmul(bank[6 + half][:, 0:TH], ones[:, :], sqs[:, 0, half * TH:(half + 1) * TH], start=True, stop=True)
                    mm.then_inc(stat_mm, 1)
                    pe.wait_ge(ln_done, GROUPS + 2)
                pe.wait_ge(bg_free, j + 1)
                part(3)

            block1(0, first=True)
            with pe.Fori(1, TILES) as j:
                block1(j)

            pe.wait_ge(tail1_done, TILES)
            pe.wait_ge(xin_free, TILES + 1)
            tf1 = tail1[:, :, :].rearrange("p r t -> p (r t)")
            for i in range(2):
                mm = transpose(bank[5][0:80, i * P:(i + 1) * P], tf1[:, i * 80:(i + 1) * 80])
            mm.then_inc(tail_t, 1)
            out_phase(OUT1, 1)

            def back(t, hb):
                rows, cols = (P, slice(t * P, (t + 1) * P)) if t < 4 else (NB, slice(SEQ, T))
                if t == 4:
                    pe.wait_ge(evac_a if hb else fin_ev, 1)
                else:
                    pe.wait_ge(out_evac, 16 + t + 1)
                pe.wait_ge(wf_done, 4 * (hb + 1))
                for k in range(4):
                    mm = transpose(bank[(2 * t + hb) % 8][0:rows, k * P:(k + 1) * P], xT[:, 4 * hb + k, cols])
                if hb:
                    mm.then_inc(fin_tr, 1)
            for t in range(4):
                back(t, 0)
            pe.wait_ge(xsum_done, 14)
            pe.wait_ge(out_evac, 20)
            for t in range(5):
                rows, cols = (P, slice(t * P, (t + 1) * P)) if t < 4 else (NB, slice(SEQ, T))
                mm = pe.matmul(bank[7][0:rows, t:t + 1], sqs[:, 0, cols], ones[:, 0:1], start=True, stop=True)
            mm.then_inc(col_sq, 1)
            for t in range(3):
                back(t, 1)
            pe.wait_ge(col_rms, 1)
            back(3, 1)
            back(4, 0)
            back(4, 1)


_INS = ["x_prompt", "x_sample", "state_ssm", "state_ssm_conv", "state_sconv", "norm_w", "final_norm_w", "ssd_w_in",
        "ssd_conv_w", "ssd_conv_b", "ssd_dt_bias", "ssd_A_log", "ssd_D", "ssd_norm_w", "ssd_w_out", "sc_w_in",
        "sc_conv_w", "sc_w_out"]
_OUTS = {"y_prompt": (1, SEQ, D), "y_sample": (NB, 1, D), "new_ssm_p": (1, 1, HEADS, HD, NS),
         "new_ssm_conv_p": (1, 1, PRE0, XBC), "new_sconv_p": (1, 1, PRE1, DI), "new_ssm_s": (1, NB, HEADS, HD, NS),
         "new_ssm_conv_s": (1, NB, PRE0, XBC), "new_sconv_s": (1, NB, PRE1, DI)}


def kernel(**inputs):
    import numpy as np
    import concourse.bacc as bacc
    from concourse.bass_utils import run_bass_kernel_spmd

    nc = bacc.Bacc("TRN2", target_bir_lowering=False, num_devices=1)
    arrays = {f"in_{n}": np.ascontiguousarray(inputs[n]) for n in _INS}
    ins = {n: nc.dram_tensor(f"in_{n}", arrays[f"in_{n}"].shape, F32, kind="ExternalInput").ap() for n in _INS}
    outs = {n: nc.dram_tensor(f"out_{n}", s, F32, kind="ExternalOutput").ap() for n, s in _OUTS.items()}
    hybrid_step(nc, ins, outs)
    r = run_bass_kernel_spmd(nc, [arrays], core_ids=[0])
    return tuple(r.results[0][f"out_{n}"] for n in _OUTS)
```
